# Optimizing a Trainium2 kernel written in Bass

```python
import jax, jax.numpy as jnp
from jax import lax
import numpy as np

D_MODEL = 2048
BATCH = 1
SEQ = 256
DEPTH = 1

MEM_LEN = 256
EPS = 1e-6
POOL_WINDOWS = (2, 4, 8, 16)
POOL_GROUP_DIM = D_MODEL // 8
POOL_DIM = POOL_GROUP_DIM * len(POOL_WINDOWS)
HGRN_DK = 128
HGRN_DV = 128
HGRN_HEADS = D_MODEL // 256
HGRN_DIM = HGRN_HEADS * HGRN_DK
MIX_DIM = POOL_DIM + HGRN_DIM
IN_DIM = POOL_DIM + 4 * HGRN_DIM
CHUNK = 64
XATTN_HEADS = 4
XATTN_HEAD_DIM = D_MODEL // XATTN_HEADS
N_GROUPS = 4
EXPERTS_PER_GROUP = 4
N_EXPERTS = N_GROUPS * EXPERTS_PER_GROUP
TOP_K_INNER = 2
D_EXPERT = D_MODEL // 4


def rmsnorm(x, gain):
    xf = x.astype(jnp.float32)
    y = xf * lax.rsqrt(jnp.mean(xf * xf, axis=-1, keepdims=True) + EPS)
    return (y * gain.astype(jnp.float32)).astype(x.dtype)

def causal_pool_mixer(u, pool_w, pool_scale):
    b, s, _ = u.shape
    uf = u.astype(jnp.float32)
    cs = jnp.concatenate([jnp.zeros((b, 1, POOL_DIM), jnp.float32), jnp.cumsum(uf, axis=1)], axis=1)
    t_plus_1 = jnp.arange(1, s + 1, dtype=jnp.int32)
    outs = []
    for g, w in enumerate(POOL_WINDOWS):
        sl = slice(g * POOL_GROUP_DIM, (g + 1) * POOL_GROUP_DIM)
        c = cs[:, :, sl]
        upper = c[:, 1:]
        lower = jnp.pad(c[:, : s + 1 - w], ((0, 0), (w - 1, 0), (0, 0)))
        count = jnp.minimum(t_plus_1, w).astype(jnp.float32)[None, :, None]
        pooled = (upper - lower) / count - uf[:, :, sl]
        outs.append(jnp.einsum('bsc,cd->bsd', pooled.astype(u.dtype), pool_w[g]))
    return (jnp.concatenate(outs, axis=-1) * pool_scale).astype(u.dtype)

def hgrn2_mixer(q_in, f_in, i_in, g_in, lb, norm_gain):
    b, s, _ = q_in.shape
    n_chunks = s // CHUNK
    q = jax.nn.silu(q_in.astype(jnp.float32))
    lb = lb.astype(jnp.float32)
    log_f = jnp.logaddexp(jnp.log(lb), jnp.log1p(-lb) + jax.nn.log_sigmoid(f_in.astype(jnp.float32)))
    k = -jnp.expm1(log_f)
    v = i_in.astype(jnp.float32)

    def to_chunks(t, d):
        return t.reshape(b, n_chunks, CHUNK, HGRN_HEADS, d).transpose(1, 0, 3, 2, 4)

    causal = jnp.tril(jnp.ones((CHUNK, CHUNK), dtype=bool))[None, None, :, :, None]

    def step(state, xs):
        qc, lfc, kc, vc = xs
        a = jnp.cumsum(lfc, axis=2)
        rel = a[:, :, :, None, :] - a[:, :, None, :, :]
        decay = jnp.exp(jnp.where(causal, rel, -jnp.inf))
        scores = jnp.einsum('bhtd,bhtsd,bhsd->bhts', qc, decay, kc)
        o = jnp.einsum('bhts,bhsv->bhtv', scores, vc) + jnp.einsum('bhtd,bhdv->bhtv', qc * jnp.exp(a), state)
        a_last = a[:, :, -1:, :]
        new_state = jnp.exp(a_last[:, :, 0, :])[..., None] * state + jnp.einsum(
            'bhsd,bhsv->bhdv', kc * jnp.exp(a_last - a), vc)
        return new_state, o

    s0 = jnp.zeros((b, HGRN_HEADS, HGRN_DK, HGRN_DV), jnp.float32)
    _, o = lax.scan(step, s0, (to_chunks(q, HGRN_DK), to_chunks(log_f, HGRN_DK),
                               to_chunks(k, HGRN_DK), to_chunks(v, HGRN_DV)))
    o = o.transpose(1, 0, 3, 2, 4).reshape(b, s, HGRN_HEADS, HGRN_DV)
    o = rmsnorm(o, norm_gain)
    gate = jax.nn.silu(g_in.astype(jnp.float32)).reshape(b, s, HGRN_HEADS, HGRN_DV)
    return (o * gate).reshape(b, s, HGRN_HEADS * HGRN_DV).astype(q_in.dtype)

def memory_cross_attention(h, mem_n, wq, wk, wv, wo):
    b, s, _ = h.shape
    m = mem_n.shape[1]
    q = (h @ wq).reshape(b, s, XATTN_HEADS, XATTN_HEAD_DIM)
    k = (mem_n @ wk).reshape(b, m, XATTN_HEADS, XATTN_HEAD_DIM)
    v = (mem_n @ wv).reshape(b, m, XATTN_HEADS, XATTN_HEAD_DIM)
    scores = jnp.einsum('bshd,bmhd->bhsm', q, k).astype(jnp.float32) * (XATTN_HEAD_DIM ** -0.5)
    p = jax.nn.softmax(scores, axis=-1).astype(v.dtype)
    o = jnp.einsum('bhsm,bmhd->bshd', p, v).reshape(b, s, D_MODEL)
    return o @ wo

def hierarchical_moe(h, router_group, router_expert, w_gate, w_up, w_down):
    b, s, _ = h.shape
    p_group = jax.nn.softmax(jnp.einsum('bsd,dg->bsg', h, router_group).astype(jnp.float32), axis=-1)
    pg_top, g_idx = lax.top_k(p_group, 1)
    logits_e = jnp.einsum('bsd,de->bse', h, router_expert).astype(jnp.float32)
    logits_e = logits_e.reshape(b, s, N_GROUPS, EXPERTS_PER_GROUP)
    g_onehot = jax.nn.one_hot(g_idx[..., 0], N_GROUPS, dtype=jnp.float32)
    sel = jnp.einsum('bsg,bsge->bse', g_onehot, logits_e)
    top_vals, top_idx = lax.top_k(sel, TOP_K_INNER)
    w_inner = jax.nn.softmax(top_vals, axis=-1)
    expert_id = g_idx * EXPERTS_PER_GROUP + top_idx
    combine = jnp.sum(jax.nn.one_hot(expert_id, N_EXPERTS, dtype=jnp.float32)
                      * (pg_top * w_inner)[..., None], axis=2).astype(h.dtype)
    y = jnp.zeros_like(h)
    for e in range(N_EXPERTS):
        hid = jax.nn.silu(h @ w_gate[e]) * (h @ w_up[e])
        y = y + combine[..., e:e + 1] * (hid @ w_down[e])
    return y

def first_inputs(seed: int = 0) -> dict:
    key = jax.random.key(seed)
    ks = jax.random.split(key, 24)
    f32 = jnp.float32

    def nrm(k, shape, scale):
        return jax.random.normal(k, shape, f32) * scale

    def gain(k, shape):
        return 1.0 + 0.02 * jax.random.normal(k, shape, f32)

    return {
        "x": nrm(ks[0], (BATCH, SEQ, D_MODEL), 1.0),
        "mem": nrm(ks[1], (BATCH, MEM_LEN, D_MODEL), 1.0),
        "norm_mix": gain(ks[2], (DEPTH, D_MODEL)),
        "w_in": nrm(ks[3], (DEPTH, D_MODEL, IN_DIM), D_MODEL ** -0.5),
        "pool_w": nrm(ks[4], (DEPTH, len(POOL_WINDOWS), POOL_GROUP_DIM, POOL_GROUP_DIM), POOL_GROUP_DIM ** -0.5),
        "pool_scale": gain(ks[5], (DEPTH, POOL_DIM)),
        "hgrn_lb_logits": nrm(ks[6], (DEPTH + 1, HGRN_DIM), 0.5),
        "hgrn_norm": gain(ks[7], (DEPTH, HGRN_DV)),
        "w_out": nrm(ks[8], (DEPTH, MIX_DIM, D_MODEL), MIX_DIM ** -0.5),
        "norm_xattn": gain(ks[9], (DEPTH, D_MODEL)),
        "norm_mem": gain(ks[10], (DEPTH, D_MODEL)),
        "xattn_wq": nrm(ks[11], (DEPTH, D_MODEL, D_MODEL), D_MODEL ** -0.5),
        "xattn_wk": nrm(ks[12], (DEPTH, D_MODEL, D_MODEL), D_MODEL ** -0.5),
        "xattn_wv": nrm(ks[13], (DEPTH, D_MODEL, D_MODEL), D_MODEL ** -0.5),
        "xattn_wo": nrm(ks[14], (DEPTH, D_MODEL, D_MODEL), D_MODEL ** -0.5),
        "norm_ffn": gain(ks[15], (DEPTH, D_MODEL)),
        "router_group": nrm(ks[16], (DEPTH, D_MODEL, N_GROUPS), D_MODEL ** -0.5),
        "router_expert": nrm(ks[17], (DEPTH, D_MODEL, N_EXPERTS), D_MODEL ** -0.5),
        "w_gate": nrm(ks[18], (DEPTH, N_EXPERTS, D_MODEL, D_EXPERT), D_MODEL ** -0.5),
        "w_up": nrm(ks[19], (DEPTH, N_EXPERTS, D_MODEL, D_EXPERT), D_MODEL ** -0.5),
        "w_down": nrm(ks[20], (DEPTH, N_EXPERTS, D_EXPERT, D_MODEL), D_EXPERT ** -0.5),
        "norm_final": gain(ks[21], (D_MODEL,)),
    }

def first_block(x, mem, norm_mix, w_in, pool_w, pool_scale, hgrn_lb_logits, hgrn_norm, w_out,
              norm_xattn, norm_mem, xattn_wq, xattn_wk, xattn_wv, xattn_wo, norm_ffn,
              router_group, router_expert, w_gate, w_up, w_down, norm_final):
    lower_bounds = jnp.cumsum(jax.nn.softmax(hgrn_lb_logits.astype(jnp.float32), axis=0), axis=0)
    splits = [POOL_DIM, POOL_DIM + HGRN_DIM, POOL_DIM + 2 * HGRN_DIM, POOL_DIM + 3 * HGRN_DIM]
    for l in range(DEPTH):
        h = rmsnorm(x, norm_mix[l])
        proj = h @ w_in[l]
        u, q_in, f_in, i_in, g_in = jnp.split(proj, splits, axis=-1)
        pool_out = causal_pool_mixer(u, pool_w[l], pool_scale[l])
        hgrn_out = hgrn2_mixer(q_in, f_in, i_in, g_in, lower_bounds[l], hgrn_norm[l])
        x = x + jnp.concatenate([pool_out, hgrn_out], axis=-1) @ w_out[l]
        h = rmsnorm(x, norm_xattn[l])
        m = rmsnorm(mem, norm_mem[l])
        x = x + memory_cross_attention(h, m, xattn_wq[l], xattn_wk[l], xattn_wv[l], xattn_wo[l])
        h = rmsnorm(x, norm_ffn[l])
        x = x + hierarchical_moe(h, router_group[l], router_expert[l], w_gate[l], w_up[l], w_down[l])
    return rmsnorm(x, norm_final)


DEPTH_2 = 2

MIX_A = D_MODEL
MIX_B = D_MODEL
MIX = MIX_A + MIX_B
H_A = 8
DV_A = MIX_A // H_A
DK_A = DV_A // 2
QK_A = H_A * DK_A
H_B = 8
DB = MIX_B // H_B
CONV_W = 4
LRU_C = 8.0
SEG_SIZES = [2 * QK_A, MIX_A, MIX_A, MIX_A, H_A, H_A, MIX_B, MIX_B]
SPLIT_AT = [int(s) for s in np.cumsum(SEG_SIZES)[:-1]]
N_IN = int(sum(SEG_SIZES))


def rms_norm(x, g):
    x32 = x.astype(jnp.float32)
    y = x32 * lax.rsqrt(jnp.mean(x32 * x32, axis=-1, keepdims=True) + EPS)
    return (y * g.astype(jnp.float32)).astype(x.dtype)

def causal_dwconv(x, w):
    c = x.shape[-1]
    return lax.conv_general_dilated(
        x, w[:, None, :].astype(x.dtype), window_strides=(1,), padding=[(CONV_W - 1, 0)],
        dimension_numbers=("NWC", "WIO", "NWC"), feature_group_count=c)

def mlstm_chunkwise(q, k, v, i_pre, log_f):
    b_, s_, h_, dk = q.shape
    dv = v.shape[-1]
    nc = s_ // CHUNK

    def chunks(t):
        return t.reshape(b_, nc, CHUNK, h_, t.shape[-1]).transpose(1, 0, 3, 2, 4)

    def gchunks(t):
        return t.reshape(b_, nc, CHUNK, h_).transpose(1, 0, 3, 2)

    causal = jnp.tril(jnp.ones((CHUNK, CHUNK), dtype=bool))

    def step(carry, xs):
        c_st, n_st, m_st = carry
        qc, kc, vc, ic, fc = xs
        bcum = jnp.cumsum(fc, axis=-1)
        dmat = jnp.where(causal, bcum[..., :, None] - bcum[..., None, :] + ic[..., None, :], -jnp.inf)
        inter = bcum + m_st[..., None]
        m_t = jnp.maximum(inter, jnp.max(dmat, axis=-1))
        w_inter = jnp.exp(inter - m_t)
        sc = jnp.einsum("bhtk,bhsk->bhts", qc, kc) * jnp.exp(dmat - m_t[..., None])
        num = jnp.einsum("bhts,bhsv->bhtv", sc, vc) + w_inter[..., None] * jnp.einsum("bhtk,bhkv->bhtv", qc, c_st)
        den = jnp.sum(sc, axis=-1) + w_inter * jnp.einsum("bhtk,bhk->bht", qc, n_st)
        hc = num / jnp.maximum(jnp.abs(den), jnp.exp(-m_t))[..., None]
        b_last = bcum[..., -1]
        g = b_last[..., None] - bcum + ic
        m_new = jnp.maximum(b_last + m_st, jnp.max(g, axis=-1))
        decay = jnp.exp(b_last + m_st - m_new)
        wk = jnp.exp(g - m_new[..., None])
        c_new = decay[..., None, None] * c_st + jnp.einsum("bhs,bhsk,bhsv->bhkv", wk, kc, vc)
        n_new = decay[..., None] * n_st + jnp.einsum("bhs,bhsk->bhk", wk, kc)
        return (c_new, n_new, m_new), hc

    init = (jnp.zeros((b_, h_, dk, dv), jnp.float32),
            jnp.zeros((b_, h_, dk), jnp.float32),
            jnp.zeros((b_, h_), jnp.float32))
    _, hs = lax.scan(step, init, (chunks(q), chunks(k), chunks(v), gchunks(i_pre), gchunks(log_f)))
    return hs.transpose(1, 0, 3, 2, 4).reshape(b_, s_, h_, dv)

def rg_lru(x, w_a, b_a, w_x, b_x, lam):
    b_, s_, _ = x.shape
    xh = x.reshape(b_, s_, H_B, DB)
    r = jax.nn.sigmoid(jnp.einsum("bshi,hij->bshj", xh, w_a.astype(jnp.float32)).reshape(b_, s_, MIX_B)
                       + b_a.astype(jnp.float32))
    i = jax.nn.sigmoid(jnp.einsum("bshi,hij->bshj", xh, w_x.astype(jnp.float32)).reshape(b_, s_, MIX_B)
                       + b_x.astype(jnp.float32))
    log_a = -LRU_C * r * jax.nn.softplus(-lam.astype(jnp.float32))
    a = jnp.exp(log_a)
    u = x * i * jnp.sqrt(-jnp.expm1(2.0 * log_a))

    def combine(left, right):
        a1, h1 = left
        a2, h2 = right
        return a1 * a2, a2 * h1 + h2

    _, h = lax.associative_scan(combine, (a, u), axis=1)
    return h

def hybrid_layer(x, norm_g, w_in, i_bias, f_bias, qk_conv, head_norm_g,
                 lru_conv_w, lru_conv_b, w_a, b_a, w_x, b_x, lam, w_out):
    b_, s_, _ = x.shape
    f32 = jnp.float32
    u = rms_norm(x, norm_g)
    p = u @ w_in
    qk, v, o, z_a, ig, fg, xb, z_b = jnp.split(p, SPLIT_AT, axis=-1)

    qk = jax.nn.silu(causal_dwconv(qk, qk_conv))
    q, k = jnp.split(qk, 2, axis=-1)
    q = q.reshape(b_, s_, H_A, DK_A).astype(f32)
    k = k.reshape(b_, s_, H_A, DK_A).astype(f32) * (DK_A ** -0.5)
    v = v.reshape(b_, s_, H_A, DV_A).astype(f32)
    i_pre = ig.astype(f32) + i_bias.astype(f32)
    log_f = jax.nn.log_sigmoid(fg.astype(f32) + f_bias.astype(f32))
    h = mlstm_chunkwise(q, k, v, i_pre, log_f)
    h = h * jax.nn.sigmoid(o.astype(f32)).reshape(b_, s_, H_A, DV_A)
    mu = jnp.mean(h, axis=-1, keepdims=True)
    var = jnp.mean(jnp.square(h - mu), axis=-1, keepdims=True)
    h = ((h - mu) * lax.rsqrt(var + EPS)).reshape(b_, s_, MIX_A) * head_norm_g.astype(f32)
    y_a = h.astype(x.dtype) * jax.nn.silu(z_a)

    xc = causal_dwconv(xb, lru_conv_w) + lru_conv_b
    y_b = rg_lru(xc.astype(f32), w_a, b_a, w_x, b_x, lam).astype(x.dtype) * jax.nn.silu(z_b)

    return x + jnp.concatenate([y_a, y_b], axis=-1) @ w_out

def second_inputs(seed: int = 0) -> dict:
    key = jax.random.key(seed)
    ks = jax.random.split(key, 20)
    f32 = jnp.float32
    n = lambda k, shp: jax.random.normal(k, shp, f32)
    u_lam = jax.random.uniform(ks[13], (DEPTH_2, MIX_B), f32, 0.9, 0.999)
    s_lam = u_lam ** (1.0 / LRU_C)
    return {
        "x": n(ks[0], (BATCH, SEQ, D_MODEL)),
        "norm_g": 1.0 + 0.02 * n(ks[1], (DEPTH_2, D_MODEL)),
        "w_in": n(ks[2], (DEPTH_2, D_MODEL, N_IN)) * (D_MODEL ** -0.5),
        "i_bias": 0.1 * n(ks[3], (DEPTH_2, H_A)),
        "f_bias": jnp.linspace(3.0, 6.0, H_A, dtype=f32)[None, :] + 0.1 * n(ks[4], (DEPTH_2, H_A)),
        "qk_conv": n(ks[5], (DEPTH_2, CONV_W, 2 * QK_A)) * (CONV_W ** -0.5),
        "head_norm_g": 1.0 + 0.02 * n(ks[6], (DEPTH_2, MIX_A)),
        "lru_conv_w": n(ks[7], (DEPTH_2, CONV_W, MIX_B)) * (CONV_W ** -0.5),
        "lru_conv_b": 0.02 * n(ks[8], (DEPTH_2, MIX_B)),
        "w_a": n(ks[9], (DEPTH_2, H_B, DB, DB)) * (DB ** -0.5),
        "b_a": 0.02 * n(ks[10], (DEPTH_2, MIX_B)),
        "w_x": n(ks[11], (DEPTH_2, H_B, DB, DB)) * (DB ** -0.5),
        "b_x": 0.02 * n(ks[12], (DEPTH_2, MIX_B)),
        "lam": jnp.log(s_lam) - jnp.log1p(-s_lam),
        "w_out": n(ks[14], (DEPTH_2, MIX, D_MODEL)) * (MIX ** -0.5),
        "final_g": 1.0 + 0.02 * n(ks[15], (D_MODEL,)),
    }

def second_block(x, norm_g, w_in, i_bias, f_bias, qk_conv, head_norm_g,
              lru_conv_w, lru_conv_b, w_a, b_a, w_x, b_x, lam, w_out, final_g):
    for l in range(DEPTH_2):
        x = hybrid_layer(x, norm_g[l], w_in[l], i_bias[l], f_bias[l], qk_conv[l], head_norm_g[l],
                         lru_conv_w[l], lru_conv_b[l], w_a[l], b_a[l], w_x[l], b_x[l], lam[l], w_out[l])
    return rms_norm(x, final_g)


def setup_inputs(seed=0):
    out = dict(first_inputs(seed))
    for name, value in second_inputs(seed + 1).items():
        if name != "x":
            out[name + "_2"] = value
    return out


def reference(
    x, mem, norm_mix, w_in, pool_w, pool_scale, hgrn_lb_logits, hgrn_norm, w_out, norm_xattn,
    norm_mem, xattn_wq, xattn_wk, xattn_wv, xattn_wo, norm_ffn, router_group, router_expert,
    w_gate, w_up, w_down, norm_final, norm_g_2, w_in_2, i_bias_2, f_bias_2, qk_conv_2,
    head_norm_g_2, lru_conv_w_2, lru_conv_b_2, w_a_2, b_a_2, w_x_2, b_x_2, lam_2, w_out_2,
    final_g_2,
):
    x = first_block(
        x, mem, norm_mix, w_in, pool_w, pool_scale, hgrn_lb_logits, hgrn_norm, w_out,
        norm_xattn, norm_mem, xattn_wq, xattn_wk, xattn_wv, xattn_wo, norm_ffn, router_group,
        router_expert, w_gate, w_up, w_down, norm_final,
    )
    return second_block(
        x, norm_g_2, w_in_2, i_bias_2, f_bias_2, qk_conv_2, head_norm_g_2, lru_conv_w_2,
        lru_conv_b_2, w_a_2, b_a_2, w_x_2, b_x_2, lam_2, w_out_2, final_g_2,
    )


_drawn_inputs = setup_inputs


def setup_inputs(seed=0):
    import zlib

    import numpy as np

    out = dict(_drawn_inputs(seed))
    spreads = {}
    factors = {'norm_xattn': 3.342,
     'norm_mem': 5.196,
     'norm_ffn': 2.679,
     'i_bias_2': 49.152,
     'head_norm_g_2': 4.895,
     'b_a_2': 64.0,
     'b_x_2': 38.924,
     'final_g_2': 8.478}
    for name, (base, spread) in spreads.items():
        noise = np.random.default_rng([zlib.crc32(name.encode()), seed]).standard_normal(out[name].shape)
        drawn = base * np.exp(spread * noise) if base else spread * noise
        out[name] = __import__('jax').numpy.asarray(drawn.astype(out[name].dtype))
    for name, factor in factors.items():
        out[name] = (out[name] * factor).astype(out[name].dtype)
    return out
```

```python
from contextlib import ExitStack

import concourse.bass as bass
from concourse import mybir

ALU = mybir.AluOpType
ACT = mybir.ActivationFunctionType
AX = mybir.AxisListType
F32 = mybir.dt.float32
F32R = mybir.dt.float32r
I32 = mybir.dt.int32
U8 = mybir.dt.uint8

P = 128
S = 256
TT = S // P
D = 2048
KT = D // P
EPS = 1e-6
COLS = 512
HEADS = 8
DK = 128
XHEADS = 4
XD = D // XHEADS
GROUPS = 4
PER_GROUP = 4
EXPERTS = GROUPS * PER_GROUP
POOL_WINDOWS = (2, 4, 8, 16)
LRU_C = 8.0
CONV_W = 4
LAYERS = 2
LEVELS = 8

CHUNKS = 4
HALVES = 2 * CHUNKS
HSLOTS = 4
RAW_FREE = HALVES
HALF_FREE = HSLOTS
PAIR_FREE = 1

U0, Q0, F0, I0, G0 = 0, 1024, 2048, 3072, 4096
QK2, V2, O2, ZA2, IG2, FG2, XB2, ZB2 = 0, 2048, 4096, 6144, 8192, 8200, 8208, 10256


class Steps:

    def __init__(self, eng, sem):
        self.eng, self.sem, self.n = eng, sem, 0

    def __call__(self, ins):
        ins.then_inc(self.sem, 1)
        self.n += 1
        return ins

    def wait(self):
        self.eng.wait_ge(self.sem, self.n)


def vec_table():
    rows, tiles, at = {}, [], 0
    def put(name, n):
        nonlocal at
        rows[name] = (len(tiles), at)
        at += n
    for n, c in (("norm_mix", 16), ("norm_xattn", 16), ("norm_mem", 16), ("norm_ffn", 16),
                 ("pool_scale", 8), ("lb0", 8), ("lb1", 8), ("hgrn_norm", 1)):
        put(n, c)
    tiles.append(at)
    at = 0
    for l in range(LAYERS):
        put(f"qk_conv{l}", 64)
        put(f"lru_conv{l}", 64)
        tiles.append(at)
        at = 0
        for n in ("norm", "lru_b", "b_a", "b_x", "lam", "head_norm"):
            put(f"{n}{l}", 16)
        tiles.append(at)
        at = 0
    return rows, tiles


def program(nc, t, out):
    with ExitStack() as ctx:
        def sb(name, shape, dt=F32):
            return ctx.enter_context(nc.sbuf_tensor(name, shape, dt))

        def sem(name):
            return ctx.enter_context(nc.semaphore(name))

        raw = sb("raw", [P, CHUNKS, 4, COLS])
        w_hi = sb("w_hi", [P, HSLOTS, 2, COLS], F32R)
        w_lo = sb("w_lo", [P, HSLOTS, 2, COLS], F32R)
        x = sb("x", [P, TT, D])
        a_hi = sb("a_hi", [P, KT, S], F32R)
        a_lo = sb("a_lo", [P, KT, S], F32R)
        b_hi = sb("b_hi", [P, KT, S], F32R)
        b_lo = sb("b_lo", [P, KT, S], F32R)
        SC = sb("scratch", [P, 13584])
        pick_r = sb("pick", [P, TT, S], F32R)
        rows_at, row_tiles = vec_table()
        vecs = sb("vecs", [P, len(row_tiles), P])
        ident = sb("ident", [P, P])
        causal = sb("causal", [P, P])
        xor_f = sb("xor_f", [P, P])
        lvl_mask = sb("lvl_mask", [P, LEVELS - 1, P], U8)
        ones = sb("ones", [P, S])
        small = sb("small", [P, 736])

        pairs = ctx.enter_context(nc.psum_tensor("pairs", [P, 2, TT, COLS], F32))
        misc = ctx.enter_context(nc.psum_tensor("misc", [P, 4, 512], F32))

        kT_dram = nc.dram_tensor("mem_keys", (XHEADS, P, 4 * S), F32).ap()
        v_dram = nc.dram_tensor("mem_values", (XHEADS, P, TT * XD), F32).ap()
        pooled_dram = nc.dram_tensor("pooled_spill", (P, 8 * S), F32).ap()

        small_at = [0]

        def tiny(n):
            at = small_at[0]
            small_at[0] += n
            assert small_at[0] <= 736
            return small[:, at:at + n]

        sq_part = tiny(8).rearrange("p (t j) -> p t j", t=TT)
        var = tiny(2)
        rstd = tiny(4).rearrange("p (e t) -> p e t", t=TT)
        neg_half = tiny(1)
        lb = tiny(8)
        omlb = tiny(8)
        lam_c = tiny(2 * 16).rearrange("p (l c) -> p l c", l=LAYERS)
        lam_p = tiny(2 * 16).rearrange("p (l c) -> p l c", l=LAYERS)
        lam_t = [tiny(2 * 16).rearrange("p (l c) -> p l c", l=LAYERS) for _ in range(6)]
        ss16 = tiny(16)
        rs16 = tiny(16)
        mx = tiny(2)
        nmx = tiny(2)
        psumv = tiny(2)
        rsum = tiny(2)
        comb = tiny(2 * EXPERTS).rearrange("p (t e) -> p t e", t=TT)
        igfg = tiny(2 * 16).rearrange("p (t c) -> p t c", t=TT)
        uecol = tiny(4 * 8).rearrange("p (g t h) -> p g t h", g=2, t=TT)
        ucol, ecol = uecol[:, 0], uecol[:, 1]
        den4 = tiny(4).rearrange("p (t h) -> p t h", t=TT)
        rden4 = tiny(4).rearrange("p (t h) -> p t h", t=TT)
        bn = tiny(4 * 6).rearrange("p (a b) -> p a b", a=4)
        mv4 = tiny(4 * 2).rearrange("p (a b) -> p a b", a=4)
        ve4 = tiny(4)
        rs4 = tiny(4)
        gate_bias = tiny(4)
        rt_l = tiny(40).rearrange("p (t c) -> p t c", t=TT)
        rt_rank = tiny(4)
        rt_m, rt_m2, rt_m3, rt_dm, rt_w, rt_w1, rt_w2, rt_pg = (tiny(2) for _ in range(8))
        rt_gd, rt_ge, rt_og, rt_sel, rt_t, rt_o1, rt_o2 = (
            tiny(8).rearrange("p (t c) -> p t c", t=TT) for _ in range(7))

        def sc(at, *shape):
            n = 1
            for s in shape:
                n *= s
            ap = SC[:, at:at + n]
            if len(shape) == 2:
                return ap.rearrange("p (a b) -> p a b", a=shape[0])
            if len(shape) == 3:
                return ap.rearrange("p (a b c) -> p a b c", a=shape[0], b=shape[1])
            return ap

        xf = x[:].rearrange("p t d -> p (t d)")
        row_stage = sc(0, 5, P)
        iota_s = SC[:, 640:768].bitcast(I32)
        iota_t = SC[:, 768:896].bitcast(I32)
        iota_x = SC[:, 896:1024].bitcast(I32)
        iota_1 = SC[:, 1024:1024 + S].bitcast(I32)
        junk = SC[:, 1536:1536 + COLS]
        kb = sc(0, HEADS, S)
        ab = sc(2048, HEADS, S)
        qb = sc(4096, HEADS, S)
        vb = sc(6144, TT, 1024)
        scb = sc(8192, 3, HEADS, P)
        gb = xf[:, 0:2048].rearrange("p (t c) -> p t c", t=TT)
        X = xf[:, 2048:4096].rearrange("p (h t) -> p h t", h=HEADS)
        Xflat = xf[:, 2048:4096]
        memx = sc(8192, TT, D)
        xs_first = sc(4096, 2, TT, COLS)
        u_sb = sc(11264 + 1024, 4, S)
        win_a = sc(6144, 2, S)
        win_b = sc(6656, 2, S)
        inv = sc(7168, 4, S)
        kv_stage = sc(11264, 2, 4 * S)
        yo = sc(0, 16, P)
        pooled_in = sc(2048, 8, S)
        pool_w = sc(4096, 8, S)
        xs_late = sc(0, 2, TT, COLS)
        qh = sc(2048, 2, 4 * S)
        kh = sc(4096, 2, 4 * S)
        vh = sc(6144, 2, TT * XD)
        prob = sc(8192, TT, S)
        probT = sc(8704, TT, S)
        gs = sc(2048, 4 * S)
        hid = sc(3072, 4 * S)
        w_rt = sc(4096, KT, 20)
        gain_b = sc(6144, D)
        pick = pick_r[:].bitcast(F32)
        place = sc(512, TT, S)
        xs_all = sc(8192, 4, TT, COLS)
        SPLIT = 3
        xt_hi, xt_lo = ([tile[:, 4 + 4 * c:8 + 4 * c, :].rearrange("p k t -> p (k t)")
                         .rearrange("p (t c) -> p t c", t=TT) for c in range(SPLIT)]
                        for tile in (b_hi, b_lo))
        upto = sc(12288, P)
        slot_i = SC[:, 12416:12416 + S].bitcast(I32)
        slot_f = sc(12672, S)
        chosen = sc(12928, TT, EXPERTS)
        slot_of = sc(12960, TT, EXPERTS + 1)
        crowded = SC[:, 12994:12995].bitcast(I32)
        fullest = sc(12995, 1)
        qm = sc(0, HEADS, S)
        km = sc(2048, HEADS, S)
        XP = sc(4096, 4, S + CONV_W - 1)
        xc = sc(5136, 4, S)
        Rb = sc(6160, 4, S)
        Ib = sc(7184, 4, S)
        Ab = sc(8208, 4, S)
        Tb = sc(9232, 4, S)
        Zb = sc(10256, 4, S)
        w_ax = sc(11280, 2, 4, S)
        w_if = sc(13328, KT, 16)
        vx = sc(4096, TT, 2, S + 1)
        so = sc(5136, TT, COLS)
        sz = sc(6160, TT, COLS)
        Wd = sc(7184, 2, 384)
        scW = sc(7952, 2, 384)
        hh = sc(8720, TT, COLS)
        row0 = 9744
        R_I, R_F, R_A, R_B, R_U, R_M, R_E = range(7)
        rowv = SC[0:8, row0:row0 + 7 * S].rearrange("p (a b) -> p a b", a=7)
        sel = SC[0:8, row0 + 7 * S:row0 + 7 * S + 8 * P].rearrange("p (h c) -> p h c", h=8)
        gain_e = sc(2048, D)
        Dm = sc(12560, 2, 384)

        landed = [sem(f"landed{i}") for i in range(CHUNKS)]
        hi_done = sem("hi_done")
        lo_done = sem("lo_done")
        used = sem("used")
        pair_read = [sem(f"pair_read{i}") for i in range(2)]
        act_s = sem("act_s")
        dve_s = sem("dve_s")
        pool_s = sem("pool_s")
        in_x = sem("in_x")
        in_mem = sem("in_mem")
        in_rows = sem("in_rows")
        in_small = sem("in_small")
        consts = sem("consts")
        rows_t = sem("rows_t")
        vecs_ok = sem("vecs_ok")
        squares = sem("squares")
        var_ok = sem("var_ok")
        rstd_ok = sem("rstd_ok")
        xs_ok = sem("xs_ok")
        turned = sem("turned")
        n_hi = sem("n_hi")
        n_lo = sem("n_lo")
        lb_sig = sem("lb_sig")
        lam_a = sem("lam_a")
        lam_d = sem("lam_d")
        lam_ok = sem("lam_ok")
        win_ok = sem("win_ok")
        pooled_out = sem("pooled_out")
        sig_ok = sem("sig_ok")
        f_ok = sem("f_ok")
        logf_ok = sem("logf_ok")
        scan_ok = sem("scan_ok")
        sub_v = sem("sub_v")
        sub_p = sem("sub_p")
        lvl_exp = sem("lvl_exp")
        mul_v = sem("mul_v")
        mul_p = sem("mul_p")
        lvl_mm = sem("lvl_mm")
        lvl_sel = sem("lvl_sel")
        o_mm = sem("o_mm")
        o_sq = sem("o_sq")
        o_ss = sem("o_ss")
        o_rs = sem("o_rs")
        o_y = sem("o_y")
        o_t = sem("o_t")
        m_hi = sem("m_hi")
        m_lo = sem("m_lo")
        pw_in = sem("pw_in")
        pw_mm = sem("pw_mm")
        kv_out = [sem(f"kv_out{i}") for i in range(2)]
        x_back = sem("x_back")
        kv_in = [sem(f"kv_in{i}") for i in range(2)]
        att_sc = sem("att_sc")
        att_max = sem("att_max")
        att_exp = sem("att_exp")
        att_p = sem("att_p")
        att_t = sem("att_t")
        att_pt = sem("att_pt")
        att_o = sem("att_o")
        att_hi = sem("att_hi")
        att_lo = sem("att_lo")
        rt_in = sem("rt_in")
        rt_mm = sem("rt_mm")
        rt_x = sem("rt_x")
        rt_e = sem("rt_e")
        comb_ok = sem("comb_ok")
        slots_in = sem("slots_in")
        xt_h = sem("xt_h")
        xt_l = sem("xt_l")
        chosen_ok = sem("chosen_ok")
        rank_mm = sem("rank_mm")
        slots_ok = sem("slots_ok")
        crowd_ok = sem("crowd_ok")
        pick_ok = sem("pick_ok")
        picked = sem("picked")
        pick_hi = sem("pick_hi")
        pick_lo = sem("pick_lo")
        place_mm = sem("place_mm")
        place_ok = sem("place_ok")
        hid_mm = sem("hid_mm")
        hid_hi = sem("hid_hi")
        hid_lo = sem("hid_lo")
        gain_in = sem("gain_in")
        scaled = sem("scaled")
        wax_in = sem("wax_in")
        wif_in = sem("wif_in")
        xp_ok = sem("xp_ok")
        conv_ok = sem("conv_ok")
        gates_mm = sem("gates_mm")
        gates_ok = sem("gates_ok")
        xi_ok = sem("xi_ok")
        at_ok = sem("at_ok")
        a2_ok = sem("a2_ok")
        om_ok = sem("om_ok")
        sq_ok = sem("sq_ok")
        ui_ok = sem("ui_ok")
        h_ok = sem("h_ok")
        z_ok = sem("z_ok")
        y_ok = sem("y_ok")
        lru_hi = sem("lru_hi")
        lru_lo = sem("lru_lo")
        qk_ok = sem("qk_ok")
        if_mm = sem("if_mm")
        if_sb = sem("if_sb")
        if_t = sem("if_t")
        row_a = sem("row_a")
        row_v = sem("row_v")
        col_t = sem("col_t")
        col_ok = sem("col_ok")
        bc_mm = sem("bc_mm")
        dm_ok = sem("dm_ok")
        wd_ok = sem("wd_ok")
        scw_ok = sem("scw_ok")
        num_mm = sem("num_mm")
        den_ok = sem("den_ok")
        hh_ok = sem("hh_ok")
        ve_ok = sem("ve_ok")
        rs_ok = sem("rs_ok")
        hn_ok = sem("hn_ok")
        hz_ok = sem("hz_ok")
        hz_t = sem("hz_t")
        mh_hi = sem("mh_hi")
        mh_lo = sem("mh_lo")
        stored = sem("stored")

        lb_d = sem("lb_d")
        xor_ok = sem("xor_ok")
        sel_ok = sem("sel_ok")
        inv_ok = sem("inv_ok")
        win_done = sem("win_done")
        xp_zero = sem("xp_zero")
        vx_ones = sem("vx_ones")

        def copied(eng, u):
            eng.wait_ge(pair_read[u % 2], u // 2 + PAIR_FREE + 1)

        def finished(eng, h):
            eng.wait_ge(used, h + HALF_FREE)

        ROW_LOADS = {}
        for l in (None, 0, 1):
            for name in (("norm_mix", "norm_xattn", "norm_mem", "norm_ffn", "pool_scale", "lb0", "lb1",
                          "hgrn_norm") if l is None else
                         tuple(f"{n}{l}" for n in ("qk_conv", "lru_conv", "norm", "lru_b", "b_a", "b_x",
                                                   "lam", "head_norm"))):
                tile, at = rows_at[name]
                n = 64 if "conv" in name and l is not None else \
                    {"pool_scale": 8, "lb0": 8, "lb1": 8, "hgrn_norm": 1}.get(name, 16)
                ROW_LOADS[name] = (tile, at, n)
        N_ROW_DMAS = len(ROW_LOADS)

        def row_source(name):
            if name in ("lb0", "lb1"):
                return t["hgrn_lb_logits"][int(name[2])].rearrange("(f p) -> f p", p=P)
            if name in t:
                return t[name][0].rearrange("(f p) -> f p", p=P)
            l = int(name[-1])
            src = {"qk_conv": "qk_conv_2", "lru_conv": "lru_conv_w_2", "norm": "norm_g_2",
                   "lru_b": "lru_conv_b_2", "b_a": "b_a_2", "b_x": "b_x_2", "lam": "lam_2",
                   "head_norm": "head_norm_g_2"}[name[:-1]]
            if "conv" in name:
                return t[src][l].rearrange("i (f p) -> (i f) p", p=P)
            return t[src][l].rearrange("(f p) -> f p", p=P)

        def col(name, n=0):
            tile, at = rows_at[name]
            return vecs[:, tile, at + n:at + n + 1]

        def cols(name, n):
            tile, at = rows_at[name]
            return vecs[:, tile, at:at + n]

        at_u, at_h, U, H = 0, 0, {}, {}
        def stage(name, units, halves=HALVES):
            nonlocal at_u, at_h
            U[name], H[name] = at_u, at_h
            at_u += units
            at_h += units * halves
        for name, n in (("u", 2), ("f", 2), ("q", 2), ("i", 2), ("g", 2), ("mk", 4), ("mv", 4),
                        ("wout", 4), ("wq", 4), ("wo", 4), ("moe0", 2)):
            stage(name, n)
        U["moe"], H["moe"] = at_u, at_h
        at_u += 2 * 5 * (EXPERTS - 1)
        MOE_READS = U["moe"] // 2 + PAIR_FREE
        at_h += 3 * HALVES * (EXPERTS - 1)
        stage("down", 4, 2)
        for l in range(LAYERS):
            for name, n in (("lru", 8), ("qk", 4), ("wb", 4), ("voz", 12), ("wa", 4)):
                stage(f"{name}{l}", n)

        def rowview(ap):
            return ap.rearrange("(c p) n -> p c n", p=P)

        w_in, w_out = rowview(t["w_in"][0]), rowview(t["w_out"][0])
        wq, wk, wv, wo = (rowview(t[f"xattn_{n}"][0]) for n in ("wq", "wk", "wv", "wo"))
        w_gate, w_up, w_down = (t[n][0].rearrange("e (c p) n -> p e c n", p=P)
                                for n in ("w_gate", "w_up", "w_down"))
        w_in2 = [rowview(t["w_in_2"][l]) for l in range(LAYERS)]
        w_out2 = [rowview(t["w_out_2"][l]) for l in range(LAYERS)]

        block = ctx.enter_context(nc.Block())

        @block.sync
        def _(sp):
            def chunk(c, count, src):
                sp.wait_ge(hi_done, count)
                sp.wait_ge(lo_done, count)
                sp.dma_start(raw[:, c:c + 1] if len(src.shape) == 4 else raw[:, c], src).then_inc(landed[c], 16)

            def units(h0, n, view, first):
                if n == 1:
                    for c in range(CHUNKS):
                        chunk(c, h0 + 2 * c + 2, view[:, 4 * c:4 * c + 4, first:first + COLS])
                    return
                with sp.Fori(0, n) as j:
                    for c in range(CHUNKS):
                        chunk(c, j * HALVES + (h0 + 2 * c + 2),
                              view[:, 4 * c:4 * c + 4, bass.ds(j * COLS + first, COLS)])

            units(H["u"], 2, w_in, U0)
            units(H["f"], 2, w_in, F0)
            units(H["q"], 2, w_in, Q0)
            units(H["i"], 2, w_in, I0)
            units(H["g"], 2, w_in, G0)
            units(H["mk"], 1, wk, 0)
            sp.wait_ge(pooled_out, 16 * 2)
            sp.wait_ge(lvl_mm, LEVELS + 1)
            sp.wait_ge(scan_ok, 2)
            sp.dma_start(pooled_in.rearrange("p a b -> p (a b)"), pooled_dram).then_inc(pw_in, 16)
            sp.dma_start(pool_w, t["pool_w"][0].rearrange("g (k p) n -> p (g k) n", p=P))\
              .then_inc(pw_in, 16)
            units(H["mk"] + HALVES, 3, wk, COLS)
            units(H["mv"], 4, wv, 0)
            sp.wait_ge(o_y, 1)
            sp.dma_start(x[:], t["x"][0].rearrange("(t p) d -> p t d", p=P)).then_inc(x_back, 16)
            units(H["wout"], 4, w_out, 0)
            for j in range(XHEADS):
                units(H["wq"] + j * HALVES, 1, wq, j * COLS)
                for i in range(2):
                    sp.wait_ge(kv_out[i], 16 * XHEADS)
                if j == 0:
                    sp.wait_ge(pw_mm, 1)
                if j >= 2:
                    sp.wait_ge(att_o, j - 1)
                sp.dma_start(kh[:, j % 2], kT_dram[j]).then_inc(kv_in[j % 2], 16)
                sp.dma_start(vh[:, j % 2], v_dram[j]).then_inc(kv_in[j % 2], 16)
            units(H["wo"], 4, wo, 0)
            sp.wait_ge(att_o, XHEADS)
            sp.dma_start(w_rt[:, :, 0:4], rowview(t["router_group"][0])).then_inc(rt_in, 16)
            sp.dma_start(w_rt[:, :, 4:20], rowview(t["router_expert"][0])).then_inc(rt_in, 16)
            sp.dma_start(gain_b, t["norm_final"].rearrange("(a d) -> a d", a=1)
                         .to_broadcast([P, D])).then_inc(gain_in, 16)

            def expert(h0, ww, e):
                for c in range(CHUNKS):
                    chunk(c, h0 + (2 * c + 2), ww[:, e, 4 * c:4 * c + 4, :])

            def down(h0, e):
                for n in range(CHUNKS):
                    chunk(n, h0 + (2 * n + 2), w_down[:, e, :, n * COLS:(n + 1) * COLS])

            expert(H["moe0"], w_gate, bass.ds(0, 1))
            expert(H["moe0"] + HALVES, w_up, bass.ds(0, 1))
            with sp.Fori(0, EXPERTS - 1) as e:
                expert(e * 24 + H["moe"], w_gate, bass.ds(e + 1, 1))
                for n in range(4):
                    h0 = e * 24 + (H["moe"] + 8 + 4 * n)
                    chunk(2 * n % CHUNKS, h0 + 2,
                          w_down[:, bass.ds(e, 1), :, n * COLS:(n + 1) * COLS])
                    chunk((2 * n + 1) % CHUNKS, h0 + 4,
                          w_up[:, bass.ds(e + 1, 1), 4 * n:4 * n + 4, :])
            down(H["down"], bass.ds(EXPERTS - 1, 1))
            for l in range(LAYERS):
                if l:
                    sp.wait_ge(mh_lo, 4 * l)
                sp.dma_start(w_if, w_in2[l][:, :, IG2:IG2 + 16]).then_inc(wif_in, 16)
                for j in range(4):
                    units(H[f"lru{l}"] + 2 * j * HALVES, 1, w_in2[l], XB2 + j * COLS)
                    for c in range(CHUNKS):
                        if c == 1:
                            if l or j:
                                sp.wait_ge(gates_mm, 4 * l + j)
                            for m, name in enumerate(("w_a_2", "w_x_2")):
                                sp.dma_start(w_ax[:, m], t[name][l, 2 * j:2 * j + 2]
                                             .rearrange("h (k p) n -> p (h k) n", p=P))\
                                  .then_inc(wax_in, 16)
                        chunk(c, H[f"lru{l}"] + (2 * j + 1) * HALVES + 2 * c + 2,
                              w_in2[l][:, 4 * c:4 * c + 4, ZB2 + j * COLS:ZB2 + (j + 1) * COLS])
                units(H[f"qk{l}"], 4, w_in2[l], QK2)
                with sp.Fori(0, 4) as j:
                    for c in range(CHUNKS):
                        chunk(c, j * HALVES + (H[f"wb{l}"] + 2 * c + 2),
                              w_out2[l][:, KT + 4 * c:KT + 4 * c + 4, bass.ds(j * COLS, COLS)])
                with sp.Fori(0, 4) as j:
                    for r, first in enumerate((V2, O2, ZA2)):
                        for c in range(CHUNKS):
                            chunk(c, j * (3 * HALVES) + (H[f"voz{l}"] + r * HALVES + 2 * c + 2),
                                  w_in2[l][:, 4 * c:4 * c + 4, bass.ds(j * COLS + first, COLS)])
                units(H[f"wa{l}"], 4, w_out2[l], 0)
                if l == LAYERS - 1:
                    sp.wait_ge(mh_lo, 4 * LAYERS)
                    sp.dma_start(gain_e, t["final_g_2"].rearrange("(a d) -> a d", a=1)
                                 .to_broadcast([P, D])).then_inc(gain_in, 16)
            sp.wait_ge(in_small, 64)
            sp.wait_ge(scaled, 4)
            sp.dma_start(out[0].rearrange("(t p) d -> p t d", p=P), x[:]).then_inc(stored, 16)
            sp.wait_ge(stored, 16)

        @block.tensor
        def _(pe):
            nc.tensor.sem_inc(used, HALF_FREE)
            def mm_tokens(r, hi, lo, k, s, q, last, tiles=TT):
                for T in range(tiles):
                    o = pairs[:, r, T, :]
                    tok = slice(T * P, (T + 1) * P)
                    nc.tensor.matmul(o, hi[:, k, tok], w_hi[:, s, q, :], start=k == 0, stop=False)
                    nc.tensor.matmul(o, hi[:, k, tok], w_lo[:, s, q, :], start=False, stop=False)
                    m = nc.tensor.matmul(o, lo[:, k, tok], w_hi[:, s, q, :], start=False, stop=last)
                return m

            def mm_features(r, hi, lo, k, s, q, last):
                for f in range(4):
                    o = pairs[:, r, f // 2, (f % 2) * S:(f % 2 + 1) * S]
                    fs = slice(f * P, (f + 1) * P)
                    nc.tensor.matmul(o, w_hi[:, s, q, fs], hi[:, k, :], start=(k == 0 and f % 2 == 0),
                                     stop=False, skip_group_check=True)
                    nc.tensor.matmul(o, w_hi[:, s, q, fs], lo[:, k, :], start=False, stop=False,
                                     skip_group_check=True)
                    m = nc.tensor.matmul(o, w_lo[:, s, q, fs], hi[:, k, :], start=False, stop=last,
                                         skip_group_check=True)
                return m

            def unit(u, h, r, body, hi, lo, hooks={}, need={}, halves=HALVES, first_slot=0):
                pe.wait_ge(pair_read[r], u)
                for i in range(halves):
                    if i in need:
                        pe.wait_ge(*need[i])
                    pe.wait_ge(lo_done, h + (RAW_FREE + i + 1))
                    for q in range(2):
                        k = 2 * i + q
                        m = body(r, hi, lo, k, (first_slot + i) % HSLOTS, q, k == 2 * halves - 1)
                    m.then_inc(used, 1)
                    if i in hooks:
                        hooks[i]()

            def pair_count(u):
                return u // 2 + PAIR_FREE

            def units(name, n, body, hi, lo, need={}):
                if need:
                    unit(pair_count(U[name]), H[name], 0, body, hi, lo, need=need)
                    unit(pair_count(U[name] + 1), H[name] + HALVES, 1, body, hi, lo)
                    if n == 2:
                        return
                    if n == 4:
                        for r in range(2):
                            unit(pair_count(U[name] + 2 + r), H[name] + (2 + r) * HALVES, r,
                                 body, hi, lo)
                        return
                if n == 2:
                    for r in range(2):
                        unit(pair_count(U[name] + r), H[name] + r * HALVES, r, body, hi, lo)
                    return
                with pe.Fori(0, n // 2) as j:
                    for r in range(2):
                        unit(j + pair_count(U[name] + r), j * (2 * HALVES) + (H[name] + r * HALVES),
                             r, body, hi, lo)

            def turn(N, c, src):
                n = 4 * N + c
                pe.wait_ge(xs_ok, n + 1)
                if n >= 2:
                    pe.wait_ge(n_lo, n - 1)
                for k in range(4):
                    for T in range(TT):
                        m = nc.tensor.transpose(misc[:, 2 * (n % 2) + k // 2,
                                                     (k % 2) * S + T * P:(k % 2) * S + (T + 1) * P],
                                                src[:, c if N == 3 else n % 2, T, k * P:(k + 1) * P],
                                                ident[:])
                m.then_inc(turned, 1)

            def ready(N):
                return {2 * c: (n_lo, 4 * N + c + 1) for c in range(4)}

            pe.wait_ge(consts, 1)
            pe.wait_ge(in_rows, 16 * N_ROW_DMAS)
            for i, n in enumerate(row_tiles):
                m = nc.tensor.transpose(misc[:, 0 if i < 4 else 1, (i % 4) * P:(i % 4) * P + n],
                                        row_stage[0:n, i, :], ident[0:n, 0:n])
            m.then_inc(rows_t, 1)
            pe.wait_ge(vecs_ok, 1)
            for c in range(4):
                turn(0, c, xs_first)

            need = ready(0)
            unit(pair_count(U["u"]), H["u"], 0, mm_features, a_hi, a_lo, need=need,
                 hooks={i: (lambda c=i - 4: turn(1, c, xs_first)) for i in range(4, 8)})
            unit(pair_count(U["u"] + 1), H["u"] + HALVES, 1, mm_features, a_hi, a_lo)
            units("f", 2, mm_features, a_hi, a_lo)
            units("q", 2, mm_features, a_hi, a_lo)

            def level(l):
                if l < 0:
                    copied(pe, U["q"] + 1)
                    pe.wait_ge(f_ok, 2)
                    pe.wait_ge(n_lo, 8)
                else:
                    pe.wait_ge(mul_v, l + 1)
                    pe.wait_ge(mul_p, l + 1)
                    pe.wait_ge(lvl_sel, l + 1)
                for h in range(HEADS):
                    if l == LEVELS - 1:
                        m = nc.tensor.matmul(misc[:, h // 4, (h % 4) * P:(h % 4 + 1) * P],
                                             X[:, h, 0:P], X[:, h, P:S], start=True, stop=True)
                        continue
                    for T in range(TT):
                        tok = slice(T * P, (T + 1) * P)
                        a, b = (kb, qb) if l < 0 else (X, X)
                        m = nc.tensor.matmul(misc[:, 2 * T + h // 4, (h % 4) * P:(h % 4 + 1) * P],
                                             a[:, h, tok], b[:, h, tok], start=True, stop=True)
                m.then_inc(lvl_mm, 1)

            for j, name in enumerate(("i", "g")):
                for r in range(2):
                    l = 4 * j + 2 * r
                    hooks = {1: (lambda l=l: level(l)), 5: (lambda l=l + 1: level(l))}
                    if l == 0:
                        hooks[0] = lambda: level(-1)
                    unit(pair_count(U[name] + r), H[name] + r * HALVES, r, mm_tokens, a_hi, a_lo,
                         hooks=hooks)

            def heads_out():
                pe.wait_ge(lvl_sel, LEVELS + 1)
                copied(pe, U["i"] + 1)
                for h in range(HEADS):
                    hv = slice(h * P, (h + 1) * P)
                    bank = slice((h % 4) * P, (h % 4 + 1) * P)
                    nc.tensor.matmul(misc[:, h // 4, bank], scb[:, 0, h, :], vb[:, 0, hv],
                                     start=True, stop=True)
                    nc.tensor.matmul(misc[:, 2 + h // 4, bank], scb[:, 1, h, :], vb[:, 0, hv],
                                     start=True, stop=False)
                    m = nc.tensor.matmul(misc[:, 2 + h // 4, bank], scb[:, 2, h, :], vb[:, 1, hv],
                                         start=False, stop=True)
                m.then_inc(o_mm, 1)

            def heads_turn():
                pe.wait_ge(o_y, 1)
                for h in range(HEADS):
                    for T in range(TT):
                        m = nc.tensor.transpose(
                            misc[:, h // 2, (h % 2) * S + T * P:(h % 2) * S + (T + 1) * P],
                            yo[:, T * HEADS + h, :], ident[:])
                m.then_inc(o_t, 1)

            def pool_mix():
                pe.wait_ge(pw_in, 32)
                pe.wait_ge(m_lo, 1)
                for g in range(4):
                    for f in range(2):
                        for k in range(2):
                            m = nc.tensor.matmul(
                                misc[:, g, f * S:(f + 1) * S], pool_w[:, 2 * g + k, f * P:(f + 1) * P],
                                pooled_in[:, 2 * g + k, :], start=k == 0, stop=k == 1)
                m.then_inc(pw_mm, 1)

            unit(pair_count(U["mk"]), H["mk"], 0, mm_features, b_hi, b_lo, hooks={3: heads_out},
                 need={0: (n_lo, 8)})
            unit(pair_count(U["mk"] + 1), H["mk"] + HALVES, 1, mm_features, b_hi, b_lo,
                 hooks={7: heads_turn})
            unit(pair_count(U["mk"] + 2), H["mk"] + 2 * HALVES, 0, mm_features, b_hi, b_lo,
                 hooks={7: pool_mix})
            unit(pair_count(U["mk"] + 3), H["mk"] + 3 * HALVES, 1, mm_features, b_hi, b_lo)
            units("mv", 4, mm_tokens, b_hi, b_lo)
            units("wout", 4, mm_tokens, a_hi, a_lo, need={0: (m_lo, 2)})
            for c in range(4):
                turn(2, c, xs_late)

            def scores(j):
                copied(pe, U["wq"] + j)
                pe.wait_ge(kv_in[j % 2], 32 * (j // 2 + 1))
                if j:
                    pe.wait_ge(att_exp, j)
                pe.wait_ge(n_lo, 12)
                for T in range(TT):
                    for k in range(4):
                        q = qh[:, j % 2, k * S + T * P:k * S + (T + 1) * P]
                        m = nc.tensor.matmul(misc[:, 0, T * S:(T + 1) * S], q,
                                             kh[:, j % 2, k * S:(k + 1) * S], start=k == 0, stop=k == 3)
                m.then_inc(att_sc, 1)

            def turn_probs(j):
                pe.wait_ge(att_p, j + 1)
                for M in range(TT):
                    for T in range(TT):
                        m = nc.tensor.transpose(misc[:, 1, M * S + T * P:M * S + (T + 1) * P],
                                                prob[:, T, M * P:(M + 1) * P], ident[:])
                m.then_inc(att_t, 1)

            def attend(j):
                pe.wait_ge(att_pt, j + 1)
                if j:
                    pe.wait_ge(att_lo, j)
                for d in range(4):
                    for M in range(TT):
                        m = nc.tensor.matmul(misc[:, 2 + d // 2, (d % 2) * S:(d % 2 + 1) * S],
                                             vh[:, j % 2, M * XD + d * P:M * XD + (d + 1) * P],
                                             probT[:, M, :], start=M == 0, stop=M == 1)
                m.then_inc(att_o, 1)

            for j in range(XHEADS):
                hooks = {}
                if j:
                    hooks = {3: (lambda j=j - 1: scores(j)), 5: (lambda j=j - 1: turn_probs(j)),
                             7: (lambda j=j - 1: attend(j))}
                unit(pair_count(U["wq"] + j), H["wq"] + j * HALVES, j % 2, mm_features, a_hi, a_lo,
                     need=ready(2) if j == 0 else {}, hooks=hooks)
            last = XHEADS - 1
            unit(pair_count(U["wo"]), H["wo"], 0, mm_tokens, b_hi, b_lo,
                 need={0: (att_lo, last), 6: (att_lo, XHEADS)},
                 hooks={1: lambda: scores(last), 3: lambda: turn_probs(last), 5: lambda: attend(last)})
            for r in range(1, 4):
                unit(pair_count(U["wo"] + r), H["wo"] + r * HALVES, r % 2, mm_tokens, b_hi, b_lo)
            for c in range(4):
                turn(3, c, xs_all)

            def route():
                pe.wait_ge(rt_in, 32)
                pe.wait_ge(n_lo, 16)
                for T in range(TT):
                    tok = slice(T * P, (T + 1) * P)
                    for k in range(KT):
                        nc.tensor.matmul(misc[:, 0, T * 20:(T + 1) * 20], a_hi[:, k, tok].bitcast(F32),
                                         w_rt[:, k, :], start=k == 0, stop=False)
                        m = nc.tensor.matmul(misc[:, 0, T * 20:(T + 1) * 20],
                                             a_lo[:, k, tok].bitcast(F32), w_rt[:, k, :],
                                             start=False, stop=k == KT - 1)
                m.then_inc(rt_mm, 1)

            def ranks():
                pe.wait_ge(chosen_ok, 1)
                one = ones[:, 0:P]
                nc.tensor.matmul(misc[:, 1, 0:16], upto, chosen[:, 0, :], start=True, stop=True)
                nc.tensor.matmul(misc[:, 1, 16:32], one, chosen[:, 0, :], start=True, stop=False)
                nc.tensor.matmul(misc[:, 1, 16:32], upto, chosen[:, 1, :], start=False, stop=True)
                nc.tensor.matmul(misc[:, 1, 32:48], one, chosen[:, 0, :], start=True, stop=False)
                nc.tensor.matmul(misc[:, 1, 32:48], one, chosen[:, 1, :], start=False, stop=True)\
                  .then_inc(rank_mm, 1)

            pc = pair_count

            def experts(tiles):
                def mm_slots(r, hi, lo, k, s, q, last):
                    return mm_tokens(r, hi, lo, k, s, q, last, tiles=tiles)

                def gather(e, c):
                    if c == 0:
                        pe.wait_ge(pick_ok, e + 1)
                    for k in range(4):
                        for T in range(TT):
                            o = misc[:, 2 * (c % 2) + k // 2, (k % 2) * S:(k % 2) * S + tiles * P]
                            fs = slice(k * P, (k + 1) * P)
                            first, last = T == 0, T == TT - 1
                            if c < SPLIT:
                                to = pick_r[:, T, 0:tiles * P]
                                nc.tensor.matmul(o, xt_hi[c][:, T, fs], to, start=first, stop=False)
                                m = nc.tensor.matmul(o, xt_lo[c][:, T, fs], to, start=False, stop=last)
                            else:
                                m = nc.tensor.matmul(o, xs_all[:, c, T, fs], pick[:, T, 0:tiles * P],
                                                     start=first, stop=last)
                    m.then_inc(picked, 1)

                def gather_hooks(e):
                    def chunk_hook(c):
                        if c == 1:
                            pe.wait_ge(place_ok, e)
                        if c >= 2:
                            pe.wait_ge(pick_lo, e * 4 + (c - 1))
                        gather(e, c)
                    return {2 * c + 1: (lambda c=c: chunk_hook(c)) for c in range(4)}

                def turn_pick():
                    for s in range(tiles):
                        for T in range(TT):
                            m = nc.tensor.transpose(misc[:, 2, s * S + T * P:s * S + (T + 1) * P],
                                                    pick[:, T, s * P:(s + 1) * P], ident[:])
                    m.then_inc(place_mm, 1)

                def scatter(e, count):
                    pe.wait_ge(pair_read[1], count)
                    pe.wait_ge(place_ok, e + 1)
                    pe.wait_ge(pick_lo, e * 4 + 7)
                    h = hid.rearrange("p (t c) -> p t c", t=TT)
                    for f in range(4):
                        for s in range(tiles):
                            m = nc.tensor.matmul(misc[:, f // 2, (f % 2) * S:(f % 2 + 1) * S],
                                                 h[:, s, f * P:(f + 1) * P], place[:, s, :],
                                                 start=s == 0, stop=s == tiles - 1)
                    m.then_inc(hid_mm, 1)

                def filled(e):
                    return {2 * c: (pick_lo, e * 4 + (c + 1)) for c in range(4)}

                for c in range(4):
                    if c < SPLIT:
                        pe.wait_ge(xt_l, c + 1)
                    if c >= 2:
                        pe.wait_ge(pick_lo, c - 1)
                    gather(0, c)
                def first_turn():
                    pe.wait_ge(pick_lo, 4)
                    turn_pick()
                unit(pc(U["moe0"]), H["moe0"], 0, mm_slots, a_hi, a_lo, need=filled(0),
                     hooks={6: first_turn})
                unit(pc(U["moe0"] + 1), H["moe0"] + HALVES, 1, mm_slots, a_hi, a_lo,
                     hooks=gather_hooks(1))
                with pe.Fori(0, EXPERTS - 1) as e:
                    def next_turn():
                        pe.wait_ge(pick_lo, e * 4 + 8)
                        turn_pick()
                    unit(e * 5 + MOE_READS, e * 24 + H["moe"], 0, mm_slots, a_hi, a_lo,
                         need=filled(e + 1),
                         hooks={4: lambda: scatter(e, e + MOE_READS), 7: next_turn})
                    pe.wait_ge(hid_lo, e + 1)
                    gathers = gather_hooks(e + 2)
                    for n in range(4):
                        h = e * 24 + (H["moe"] + HALVES + 4 * n)
                        unit(e * 5 + (MOE_READS + 1 + n), h, 0, mm_tokens, b_hi, b_lo, halves=2)
                        if n == 0:
                            pe.wait_ge(pair_read[1], e + MOE_READS)
                        for i in range(2):
                            pe.wait_ge(lo_done, h + (RAW_FREE + 2 + i + 1))
                            for q in range(2):
                                k = 4 * n + 2 * i + q
                                m = mm_slots(1, a_hi, a_lo, k, 2 + i, q, k == KT - 1)
                            m.then_inc(used, 1)
                        gathers[2 * n + 1]()
                scatter(EXPERTS - 1, pc(U["down"]))
                pe.wait_ge(hid_lo, EXPERTS)
                for n in range(4):
                    unit(pc(U["down"] + n), H["down"] + 2 * n, n % 2, mm_tokens, b_hi, b_lo,
                         halves=2, first_slot=2 * n)

            route()
            ranks()
            pe.wait_ge(crowd_ok, 1)
            pe.wait_ge(slots_ok, 1)
            many = nc.values_load(crowded[0:1, 0:1], engines=[pe.engine], min_val=0, max_val=P)
            with pe.If(many):
                experts(TT)
            with pe.Else():
                experts(1)

            def lru_gates(l, j, a):
                g = 4 * l + j
                pe.wait_ge(conv_ok, 8 * l + j + 1)
                pe.wait_ge(wax_in, 32 * (g + 1))
                if g:
                    pe.wait_ge(gates_ok, g)
                for m_ in range(2):
                    for f in range(2):
                        for k in range(2):
                            m = nc.tensor.matmul(misc[:, 2 * m_ + a, f * S:(f + 1) * S],
                                                 w_ax[:, m_, 2 * a + k, f * P:(f + 1) * P],
                                                 xc[:, 2 * a + k, :], start=k == 0, stop=k == 1)
                if a:
                    m.then_inc(gates_mm, 1)

            def if_gates(l):
                pe.wait_ge(wif_in, 16 * (l + 1))
                pe.wait_ge(gates_ok, 4 * (l + 1))
                for T in range(TT):
                    tok = slice(T * P, (T + 1) * P)
                    for k in range(KT):
                        nc.tensor.matmul(misc[:, 0, T * 16:(T + 1) * 16], a_hi[:, k, tok].bitcast(F32),
                                         w_if[:, k, :], start=k == 0, stop=False)
                        m = nc.tensor.matmul(misc[:, 0, T * 16:(T + 1) * 16],
                                             a_lo[:, k, tok].bitcast(F32), w_if[:, k, :],
                                             start=False, stop=k == KT - 1)
                m.then_inc(if_mm, 1)

            def if_turn(l):
                pe.wait_ge(if_sb, l + 1)
                for g in range(2):
                    for T in range(TT):
                        m = nc.tensor.transpose(misc[0:8, 1, g * S + T * P:g * S + (T + 1) * P],
                                                igfg[:, T, 8 * g:8 * g + 8], ident[:])
                m.then_inc(if_t, 1)

            def cols_turn(l):
                pe.wait_ge(row_a, 2 * (l + 1))
                pe.wait_ge(row_v, 2 * (l + 1))
                for g, r in enumerate((R_U, R_E)):
                    for T in range(TT):
                        m = nc.tensor.transpose(misc[:, 2, g * 16 + T * 8:g * 16 + T * 8 + 8],
                                                rowv[:, r, T * P:(T + 1) * P], ident[0:8, 0:8])
                m.then_inc(col_t, 1)

            def decay(l, j):
                g = 4 * l + j
                pe.wait_ge(col_ok, l + 1)
                pe.wait_ge(sel_ok, l + 1)
                pe.wait_ge(qk_ok, 4 * (l + 1))
                if g:
                    pe.wait_ge(hh_ok, g)
                for a in range(2):
                    h = 2 * j + a
                    nc.tensor.matmul(misc[:, 0, a * S:(a + 1) * S], sel[:, h, :], rowv[:, R_M, :],
                                     start=True, stop=True)
                for a in range(2):
                    h = 2 * j + a
                    nc.tensor.matmul(misc[:, 1 + a, 0:S], km[:, h, 0:P], qm[:, h, :],
                                     start=True, stop=True)
                    m = nc.tensor.matmul(misc[:, 1 + a, S:S + P], km[:, h, P:S], qm[:, h, P:S],
                                         start=True, stop=True)
                m.then_inc(bc_mm, 1)

            def numerators(l, j):
                g = 4 * l + j
                pe.wait_ge(scw_ok, g + 1)
                pe.wait_ge(vx_ones, l + 1)
                copied(pe, U[f"voz{l}"] + 3 * j)
                if g:
                    pe.wait_ge(mh_lo, g)
                for a in range(2):
                    nc.tensor.matmul(misc[:, a, 0:S + 1], scW[:, a, 0:P], vx[:, 0, a, :],
                                     start=True, stop=True)
                    nc.tensor.matmul(misc[:, 2 + a, 0:S + 1], scW[:, a, P:S], vx[:, 0, a, :],
                                     start=True, stop=False)
                    m = nc.tensor.matmul(misc[:, 2 + a, 0:S + 1], scW[:, a, S:S + P], vx[:, 1, a, :],
                                         start=False, stop=True)
                m.then_inc(num_mm, 1)

            def turn_heads(l, j):
                g = 4 * l + j
                pe.wait_ge(hz_ok, g + 1)
                if j < 3:
                    pe.wait_ge(scw_ok, g + 2)
                for k in range(4):
                    for T in range(TT):
                        m = nc.tensor.transpose(
                            misc[:, k // 2, (k % 2) * S + T * P:(k % 2) * S + (T + 1) * P],
                            hh[:, T, k * P:(k + 1) * P], ident[:])
                m.then_inc(hz_t, 1)

            for l in range(LAYERS):
                for c in range(4):
                    turn(4 + l, c, xs_late)
                for n in range(8):
                    hooks = {}
                    if n >= 2 and n % 2 == 0:
                        j = n // 2 - 1
                        hooks = {0: (lambda j=j: lru_gates(l, j, 0)), 2: (lambda j=j: lru_gates(l, j, 1))}
                    unit(pc(U[f"lru{l}"] + n), H[f"lru{l}"] + n * HALVES, n % 2, mm_features, a_hi,
                         a_lo, need=ready(4 + l) if n == 0 else {}, hooks=hooks)
                for n in range(4):
                    hooks = {}
                    if n == 0:
                        hooks = {0: lambda: lru_gates(l, 3, 0), 2: lambda: lru_gates(l, 3, 1)}
                    unit(pc(U[f"qk{l}"] + n), H[f"qk{l}"] + n * HALVES, n % 2, mm_features, a_hi,
                         a_lo, hooks=hooks)
                for n in range(4):
                    hooks = {0: {1: lambda: if_gates(l), 5: lambda: if_turn(l)},
                             1: {}, 2: {1: lambda: cols_turn(l)}, 3: {}}[n]
                    unit(pc(U[f"wb{l}"] + n), H[f"wb{l}"] + n * HALVES, n % 2, mm_tokens, b_hi, b_lo,
                         need={0: (lru_lo, 4 * (l + 1))} if n == 0 else {}, hooks=hooks)
                for j in range(4):
                    for r in range(3):
                        n = 3 * j + r
                        hooks = {}
                        if r == 0:
                            hooks = {0: lambda: decay(l, j)}
                            if j:
                                hooks[5] = lambda: turn_heads(l, j - 1)
                        if r == 2:
                            hooks = {0: lambda: numerators(l, j)}
                        unit(pc(U[f"voz{l}"] + n), H[f"voz{l}"] + n * HALVES, n % 2, mm_tokens, a_hi,
                             a_lo, hooks=hooks)
                for n in range(4):
                    unit(pc(U[f"wa{l}"] + n), H[f"wa{l}"] + n * HALVES, n % 2, mm_tokens, b_hi, b_lo,
                         need={0: (mh_lo, 4 * l + 3), 6: (mh_lo, 4 * l + 4)} if n == 0 else {},
                         hooks={5: lambda: turn_heads(l, 3)} if n == 0 else {})

        @block.gpsimd
        def _(pool):
            step = Steps(pool, pool_s)
            g = nc.gpsimd
            step(g.memset(ident[:], 0.0))
            step.wait()
            g.affine_select(out=ident[:], in_=ident[:], compare_op=ALU.not_equal, fill=1.0, base=0,
                            pattern=[[-1, P]], channel_multiplier=1).then_inc(consts, 1)
            step(g.memset(causal[:], 0.0))
            step.wait()
            g.affine_select(out=causal[:], in_=causal[:], compare_op=ALU.is_ge, fill=-1e30, base=0,
                            pattern=[[1, P]], channel_multiplier=-1).then_inc(consts, 1)
            g.memset(neg_half, -0.5)
            g.memset(ones[:], 1.0).then_inc(consts, 1)
            g.iota(iota_s, pattern=[[0, P]], base=0, channel_multiplier=1)
            g.iota(iota_t, pattern=[[1, P]], base=0, channel_multiplier=0)
            g.iota(iota_1, pattern=[[1, S]], base=1, channel_multiplier=0).then_inc(consts, 1)
            pool.wait_ge(xor_ok, 1)
            g.affine_select(out=xor_f[:], in_=xor_f[:], compare_op=ALU.is_gt, fill=0.0, base=0,
                            pattern=[[1, P]], channel_multiplier=-1).then_inc(consts, 1)

            def power(event):
                pool.wait_ge(var_ok, event + 1)
                g.tensor_tensor(rstd[:, event % 2, :], var, neg_half.to_broadcast([P, TT]),
                                ALU.pow).then_inc(rstd_ok, 1)

            power(0)
            power(1)

            for j in range(2):
                copied(pool, U["u"] + j)
                for gg in range(2):
                    wdw = POOL_WINDOWS[2 * j + gg]
                    uu = u_sb[:, 2 * gg:2 * gg + 2, :]
                    src, dst, s = uu, win_a, 1
                    while s < wdw:
                        g.tensor_copy(dst[:, :, 0:s], src[:, :, 0:s])
                        step(g.tensor_tensor(dst[:, :, s:S], src[:, :, s:S], src[:, :, 0:S - s],
                                             ALU.add))
                        step.wait()
                        src, dst, s = dst, (win_b if dst is win_a else win_a), 2 * s
                    if j == 0 and gg == 0:
                        pool.wait_ge(inv_ok, 1)
                    step(g.tensor_tensor(dst, src, inv[:, 2 * j + gg:2 * j + gg + 1, :]
                                         .to_broadcast([P, 2, S]), ALU.mult))
                    step.wait()
                    step(g.tensor_tensor(uu, dst, uu, ALU.subtract))
                step.wait()
                pool.dma_start(pooled_dram[:, j * 4 * S:(j + 1) * 4 * S],
                               u_sb.rearrange("p a b -> p (a b)")).then_inc(pooled_out, 16)
            pool.sem_inc(win_done, 1)

            for l in range(LEVELS):
                B = 1 << l
                Xv, av, kv = (z.rearrange("p h (m two b) -> p (h m) two b", two=2, b=B)
                              for z in (X, ab, kb))
                n = HEADS * S // (2 * B)
                if l == 0:
                    pool.wait_ge(scan_ok, 2)
                    pool.wait_ge(xs_ok, 4)
                else:
                    pool.wait_ge(lvl_mm, l + 1)
                g.tensor_tensor(Xv[:, :, 0, :], av[:, :, 0, B - 1:B].to_broadcast([P, n, B]),
                                av[:, :, 0, :], ALU.subtract).then_inc(sub_p, 1)
                pool.wait_ge(lvl_exp, l + 1)
                g.tensor_tensor(Xv[:, :, 0, :], Xv[:, :, 0, :], kv[:, :, 0, :],
                                ALU.mult).then_inc(mul_p, 1)
            pool.wait_ge(o_ss, 1)
            g.tensor_tensor(rs16, ss16, neg_half.to_broadcast([P, 16]), ALU.pow).then_inc(o_rs, 1)
            power(2)
            power(3)
            g.iota(slot_i, pattern=[[1, S]], base=1, channel_multiplier=0).then_inc(slots_in, 1)

            power(4)
            power(5)
            for l in range(LAYERS):
                if l:
                    pool.wait_ge(mh_lo, 4 * l)
                g.memset(XP[:, :, 0:CONV_W - 1], 0.0).then_inc(xp_zero, 1)
                for j in range(4):
                    n = 4 * l + j
                    pool.wait_ge(gates_ok, n + 1)
                    g.tensor_tensor(Ib, xc, Ib, ALU.mult).then_inc(ui_ok, 1)
                    pool.wait_ge(at_ok, n + 1)
                    g.tensor_tensor(Rb, Ab, Ab, ALU.mult).then_inc(a2_ok, 1)
                    pool.wait_ge(h_ok, n + 1)
                    copied(pool, U[f"lru{l}"] + 2 * j + 1)
                    g.tensor_tensor(Zb, Rb, Zb, ALU.mult).then_inc(y_ok, 1)
                pool.wait_ge(lru_lo, 4 * (l + 1))
                step(g.memset(sel, 0.0))
                step.wait()
                g.affine_select(out=sel, in_=sel, compare_op=ALU.not_equal, fill=1.0, base=0,
                                pattern=[[-1, HEADS], [0, P]], channel_multiplier=1)\
                 .then_inc(sel_ok, 1)
                pool.wait_ge(qk_ok, 4 * (l + 1))
                g.memset(vx[:, :, :, S:S + 1], 1.0).then_inc(vx_ones, 1)
                for j in range(4):
                    pool.wait_ge(ve_ok, 4 * l + j + 1)
                    g.tensor_tensor(rs4, ve4, neg_half.to_broadcast([P, 4]), ALU.pow)\
                     .then_inc(rs_ok, 1)
                power(6 + l)

        @block.scalar
        def _(act):
            a = nc.scalar
            step = Steps(act, act_s)
            act.dma_start(x[:], t["x"][0].rearrange("(t p) d -> p t d", p=P)).then_inc(in_x, 16)
            for name, (tile, at, n) in ROW_LOADS.items():
                act.dma_start(row_stage[at:at + n, tile, :], row_source(name)).then_inc(in_rows, 16)
            act.dma_start(memx, t["mem"][0].rearrange("(t p) d -> p t d", p=P)).then_inc(in_mem, 16)
            for l in range(LAYERS):
                for i, name in enumerate(("i_bias_2", "f_bias_2")):
                    act.dma_start(gate_bias[0:8, 2 * l + i:2 * l + i + 1],
                                  t[name][l].rearrange("(h a) -> h a", a=1)).then_inc(in_small, 16)

            state = [0]

            def run(n):
                for _ in range(n):
                    h = state[0]
                    half(h + 1, 16 * (h // HALVES + 1), h % HALVES)
                    state[0] += 1

            def half(count, load, i):
                if i % 2 == 0:
                    act.wait_ge(landed[i // 2], load)
                act.wait_ge(used, count)
                a.activation(w_hi[:, i % HSLOTS], raw[:, i // 2, 2 * (i % 2):2 * (i % 2) + 2, :],
                             ACT.Copy).then_inc(hi_done, 1)

            def bank4(u):
                return pairs[:, u % 2].rearrange("p t c -> p (t c)").rearrange("p (f t) -> p f t", f=4)

            def read(ins, u):
                ins.then_inc(pair_read[u % 2], 1)

            def done(u_name, n, h=None):
                finished(act, H[u_name] + (n + 1) * HALVES)

            def squares_of(src, j):
                for T in range(TT):
                    if step.n:
                        step.wait()
                    step(a.activation(junk, src[:, T, j * COLS:(j + 1) * COLS], ACT.Square,
                                      accum_out=sq_part[:, T, j:j + 1]))

            def squares_done():
                step.wait()
                a.sem_inc(squares, 1)

            def split_hi(N, c, dst, gain):
                n = 4 * N + c
                act.wait_ge(turned, n + 1)
                for k in range(4):
                    m = a.activation(dst[:, 4 * c + k, :],
                                     misc[:, 2 * (n % 2) + k // 2, (k % 2) * S:(k % 2 + 1) * S],
                                     ACT.Identity, scale=col(gain, 4 * c + k))
                m.then_inc(n_hi, 1)

            act.wait_ge(in_x, 16)
            for j in range(4):
                squares_of(x, j)
            squares_done()
            act.wait_ge(in_mem, 16)
            act.wait_ge(var_ok, 1)
            for j in range(4):
                squares_of(memx, j)
            squares_done()
            act.wait_ge(lb_d, 1)
            a.activation(lb, lam_t[5][:, 0, 0:8], ACT.Sigmoid)
            a.activation(omlb, lam_t[5][:, 0, 0:8], ACT.Sigmoid, scale=-1.0).then_inc(lb_sig, 1)
            act.wait_ge(lam_d, 1)
            a.activation(lam_t[1], lam_t[0], ACT.Exp, scale=-1.0).then_inc(lam_a, 1)
            act.wait_ge(vecs_ok, 1)
            for c in range(4):
                split_hi(0, c, a_hi, "norm_mix")
            act.wait_ge(lam_d, 2)
            a.activation(lam_t[3], lam_t[2], ACT.Ln).then_inc(lam_a, 1)

            run(5)
            for c in range(4):
                split_hi(1, c, b_hi, "norm_mem")
                if c < 3:
                    run(1)

            def pool_copy(j):
                u = U["u"] + j
                done("u", j)
                if j:
                    act.wait_ge(pooled_out, 16 * j)
                read(a.activation(u_sb, bank4(u), ACT.Copy), u)

            run(3); pool_copy(0); run(5)

            def f_copy(j):
                u = U["f"] + j
                done("f", j)
                a.activation(kb[:, 4 * j:4 * j + 4, :], bank4(u), ACT.Sigmoid, scale=-1.0)
                read(a.activation(ab[:, 4 * j:4 * j + 4, :], bank4(u), ACT.Sigmoid), u)

            def f_log(j):
                act.wait_ge(f_ok, j + 1)
                a.activation(ab[:, 4 * j:4 * j + 4, :], ab[:, 4 * j:4 * j + 4, :], ACT.Ln)\
                 .then_inc(logf_ok, 1)

            def silu_features(name, j, dst):
                u = U[name] + j
                done(name, j)
                read(a.activation(dst, bank4(u), ACT.Silu), u)

            def tokens_copy(name, j, dst, func):
                u = U[name] + j
                done(name, j)
                read(a.activation(dst, pairs[:, u % 2], func), u)

            def exp_level(l):
                act.wait_ge(sub_v, l + 1)
                act.wait_ge(sub_p, l + 1)
                a.activation(X, X, ACT.Exp).then_inc(lvl_exp, 1)

            run(3); pool_copy(1); run(5)
            run(3); f_copy(0); run(2); f_log(0); run(3)
            run(3); f_copy(1); run(2); f_log(1); run(3)
            run(3); silu_features("q", 0, qb[:, 0:4, :]); run(5)
            for n, (name, r) in enumerate((("i", 0), ("i", 1), ("g", 0), ("g", 1))):
                run(2); exp_level(2 * n); run(1)
                if n == 0:
                    silu_features("q", 1, qb[:, 4:8, :])
                elif n < 3:
                    if n == 1:
                        act.wait_ge(win_done, 1)
                    tokens_copy("i", n - 1, vb[:, :, (n - 1) * COLS:n * COLS], ACT.Copy)
                else:
                    tokens_copy("g", 0, gb[:, :, 0:COLS], ACT.Silu)
                run(3); exp_level(2 * n + 1); run(2)

            def stage_kv(n):
                name, j = ("mk", n) if n < 4 else ("mv", n - 4)
                u = U[name] + j
                done(name, j)
                if n >= 2:
                    act.wait_ge(kv_out[n % 2], 16 * (n // 2))
                if n == 0:
                    act.wait_ge(pooled_out, 32)
                src = bank4(u) if n < 4 else pairs[:, u % 2]
                dst = kv_stage[:, n % 2]
                shaped = dst.rearrange("p (f t) -> p f t", f=4) if n < 4 else \
                    dst.rearrange("p (t c) -> p t c", t=TT)
                read(a.activation(shaped, src, ACT.Copy), u)
                copied(act, u)
                act.dma_start(kT_dram[j] if n < 4 else v_dram[j], dst).then_inc(kv_out[n % 2], 16)

            run(3); tokens_copy("g", 1, gb[:, :, COLS:2 * COLS], ACT.Silu); run(3)
            act.wait_ge(o_mm, 1)
            a.activation(Xflat, misc[:].rearrange("p b c -> p (b c)"), ACT.Square).then_inc(o_sq, 1)
            run(2)
            run(3); stage_kv(0); run(5)
            run(3); stage_kv(1); run(1)
            act.wait_ge(o_t, 1)
            a.activation(a_hi[:, 8:16, :], misc[:].rearrange("p b (f t) -> p (b f) t", f=2),
                         ACT.Identity, scale=col("hgrn_norm")).then_inc(m_hi, 1)
            run(4)
            run(3); stage_kv(2); run(1)
            act.wait_ge(pw_mm, 1)
            for k in range(8):
                m = a.activation(a_hi[:, k, :], misc[:, k // 2, (k % 2) * S:(k % 2 + 1) * S],
                                 ACT.Identity, scale=col("pool_scale", k))
            m.then_inc(m_hi, 1)
            run(4)
            for n in range(3, 7):
                run(3); stage_kv(n); run(5)
            run(3); stage_kv(7); run(5)

            def residual_squares(name, j):
                copied(act, U[name] + j)
                squares_of(x, j)

            for i in range(2):
                act.wait_ge(kv_out[i], 16 * XHEADS)
            for j in range(3):
                run(4); residual_squares("wout", j); run(4)
            residual_squares("wout", 3)
            squares_done()
            for c in range(4):
                split_hi(2, c, a_hi, "norm_xattn")

            def q_copy(j):
                u = U["wq"] + j
                done("wq", j)
                read(a.activation(qh[:, j % 2].rearrange("p (f t) -> p f t", f=4), bank4(u),
                                  ACT.Copy), u)

            def soft_exp(j):
                act.wait_ge(att_max, j + 1)
                for T in range(TT):
                    m = a.activation(prob[:, T, :], misc[:, 0, T * S:(T + 1) * S], ACT.Exp,
                                     bias=nmx[:, T:T + 1], scale=XD ** -0.5,
                                     accum_out=psumv[:, T:T + 1])
                m.then_inc(att_exp, 1)

            def probs_back(j):
                act.wait_ge(att_t, j + 1)
                a.activation(probT, misc[:, 1].rearrange("p (m t) -> p m t", m=TT), ACT.Copy)\
                 .then_inc(att_pt, 1)

            def attended_hi(j):
                act.wait_ge(att_o, j + 1)
                a.activation(b_hi[:, 4 * j:4 * j + 4, :],
                             misc[:, 2:4].rearrange("p b (f t) -> p (b f) t", f=2), ACT.Copy)\
                 .then_inc(att_hi, 1)

            run(8)
            for j in range(1, XHEADS):
                if j >= 2:
                    run(1); attended_hi(j - 2); run(2)
                else:
                    run(3)
                q_copy(j - 1); run(2); soft_exp(j - 1); run(2); probs_back(j - 1); run(1)
            attended_hi(2)
            run(2); q_copy(3); run(1); soft_exp(3); run(2); probs_back(3); run(2); attended_hi(3)
            run(1)
            for j in range(3):
                run(4); residual_squares("wo", j); run(4)
            residual_squares("wo", 3)
            squares_done()
            for c in range(4):
                split_hi(3, c, a_hi, "norm_ffn")

            for c in range(SPLIT):
                act.wait_ge(xs_ok, 13 + c)
                a.activation(xt_hi[c], xs_all[:, c], ACT.Copy).then_inc(xt_h, 1)

            def silu_gate(r):
                a.activation(gs, pairs[:, r].rearrange("p t c -> p (t c)"), ACT.Silu)\
                 .then_inc(pair_read[r], 1)

            def hidden_hi(e):
                act.wait_ge(hid_mm, e + 1)
                a.activation(b_hi[:, 0:4, :].rearrange("p k t -> p (k t)"),
                             misc[:, 0:2].rearrange("p b c -> p (b c)"), ACT.Copy).then_inc(hid_hi, 1)

            def gathered_hi(e, c):
                act.wait_ge(picked, e * 4 + (c + 1))
                for k in range(4):
                    m = a.activation(a_hi[:, 4 * c + k, :],
                                     misc[:, 2 * (c % 2) + k // 2, (k % 2) * S:(k % 2 + 1) * S],
                                     ACT.Identity, scale=col("norm_ffn", 4 * c + k))
                m.then_inc(pick_hi, 1)

            def place_copy(e):
                act.wait_ge(place_mm, e + 1)
                a.activation(place.rearrange("p s t -> p (s t)"), misc[:, 2, :], ACT.Copy)\
                 .then_inc(place_ok, 1)

            run(4)
            act.wait_ge(rt_x, 1)
            a.activation(rt_ge, rt_gd, ACT.Exp).then_inc(rt_e, 1)
            act.wait_ge(rt_x, 2)
            a.activation(rt_w, rt_dm, ACT.Exp).then_inc(rt_e, 1)
            for c in range(4):
                gathered_hi(0, c)
            run(4)
            place_copy(0)
            run(3); done("moe0", 0); silu_gate(0)
            run(1); gathered_hi(1, 0)
            run(2); gathered_hi(1, 1)
            run(2); gathered_hi(1, 2)
            assert state[0] == H["moe"]
            h0 = H["moe"]
            with act.Fori(0, EXPERTS - 1) as e:
                def halves(first, n):
                    for i in range(first, first + n):
                        half(e * 24 + (h0 + i + 1), e * 48 + 16 * ((h0 + i) // HALVES + 1), i % HALVES)
                halves(0, 3); gathered_hi(e + 1, 3)
                halves(3, 4); hidden_hi(e)
                halves(7, 3)
                act.wait_ge(used, e * 24 + (h0 + 8 + HALF_FREE))
                act.wait_ge(pair_read[1], e + MOE_READS)
                silu_gate(0)
                place_copy(e + 1)
                halves(10, 5); gathered_hi(e + 2, 0)
                halves(15, 4); gathered_hi(e + 2, 1)
                halves(19, 4); gathered_hi(e + 2, 2)
                halves(23, 1)
            state[0] = H["down"]
            gathered_hi(EXPERTS, 3)
            hidden_hi(EXPERTS - 1)
            run(4)
            for n in range(4):
                if n < 2:
                    run(2)
                copied(act, U["down"] + n)
                squares_of(x, n)
            squares_done()
            act.wait_ge(scaled, 2)
            for j in range(4):
                squares_of(x, j)
            squares_done()

            def lru_unit(l, m_):
                todo = {i: [] for i in range(9)}
                names = [(f"lru{l}", i) for i in range(8)] + [(f"qk{l}", i) for i in range(4)] + \
                        [(f"wb{l}", i) for i in range(4)]

                def pad_copy(i):
                    name, n = (f"lru{l}", 2 * i) if i < 4 else (f"qk{l}", i - 4)
                    u = U[name] + n
                    done(name, n)
                    c = 8 * l + i
                    if c:
                        act.wait_ge(conv_ok, c)
                    if i == 0:
                        act.wait_ge(xp_zero, l + 1)
                    read(a.activation(XP[:, :, CONV_W - 1:], bank4(u), ACT.Copy), u)

                def z_silu(j):
                    n = 4 * l + j
                    if n:
                        act.wait_ge(lru_lo, n)
                    silu_features(f"lru{l}", 2 * j + 1, Zb)

                def sigmoids(j):
                    n = 4 * l + j
                    act.wait_ge(gates_mm, n + 1)
                    if n:
                        act.wait_ge(lru_lo, n)
                    for dst, b, name in ((Rb, 0, "b_a"), (Ib, 2, "b_x")):
                        for k in range(4):
                            m = a.activation(dst[:, k, :],
                                             misc[:, b + k // 2, (k % 2) * S:(k % 2 + 1) * S],
                                             ACT.Sigmoid, bias=col(f"{name}{l}", 4 * j + k))
                    m.then_inc(gates_ok, 1)

                def exps(j):
                    act.wait_ge(gates_ok, 4 * l + j + 1)
                    for k in range(4):
                        a.activation(Ab[:, k, :], Rb[:, k, :], ACT.Exp,
                                     scale=lam_c[:, l, 4 * j + k:4 * j + k + 1])
                        m = a.activation(Tb[:, k, :], Rb[:, k, :], ACT.Tanh,
                                         scale=lam_p[:, l, 4 * j + k:4 * j + k + 1])
                    m.then_inc(at_ok, 1)

                def root(j):
                    act.wait_ge(om_ok, 4 * l + j + 1)
                    a.activation(Tb, Tb, ACT.Sqrt).then_inc(sq_ok, 1)

                def y_hi(j):
                    act.wait_ge(y_ok, 4 * l + j + 1)
                    a.activation(b_hi[:, 4 * j:4 * j + 4, :], Zb, ACT.Copy).then_inc(lru_hi, 1)

                def qk_silu(n):
                    act.wait_ge(conv_ok, 8 * l + 4 + n + 1)
                    dst = (qm, km)[n // 2]
                    a.activation(dst[:, 4 * (n % 2):4 * (n % 2) + 4, :], xc, ACT.Silu)\
                     .then_inc(qk_ok, 1)

                if m_ <= 7 and m_ % 2 == 1:
                    todo[3].append(lambda: pad_copy(m_ // 2))
                if 9 <= m_ <= 12:
                    todo[3].append(lambda: pad_copy(4 + m_ - 9))
                if 2 <= m_ <= 8 and m_ % 2 == 0:
                    j = m_ // 2 - 1
                    todo[3].append(lambda: z_silu(j))
                    todo[4].append(lambda: sigmoids(j))
                    todo[6].append(lambda: exps(j))
                if 3 <= m_ <= 9 and m_ % 2 == 1:
                    j = (m_ - 3) // 2
                    todo[2].append(lambda: root(j))
                    todo[7].append(lambda: y_hi(j))
                if 10 <= m_ <= 13:
                    todo[1].append(lambda: qk_silu(m_ - 10))
                return todo

            def work(todo):
                for i in range(9):
                    for f in todo.get(i, []):
                        f()
                    if i < 8:
                        run(1)

            for l in range(LAYERS):
                for c in range(4):
                    split_hi(4 + l, c, a_hi, f"norm{l}")

                def rows_1():
                    act.wait_ge(if_t, l + 1)
                    act.wait_ge(in_small, 16 * 4)
                    a.activation(rowv[:, R_I, :], misc[0:8, 1, 0:S], ACT.Identity,
                                 bias=gate_bias[0:8, 2 * l:2 * l + 1])
                    step(a.activation(rowv[:, R_F, :], misc[0:8, 1, S:2 * S], ACT.Identity,
                                      bias=gate_bias[0:8, 2 * l + 1:2 * l + 2]))
                    step.wait()
                    step(a.activation(rowv[:, R_A, :], rowv[:, R_F, :], ACT.Abs))
                    step.wait()
                    step(a.activation(rowv[:, R_A, :], rowv[:, R_A, :], ACT.Exp, scale=-1.0))
                    step.wait()
                    a.activation(rowv[:, R_A, :], rowv[:, R_A, :], ACT.Ln, bias=1.0)\
                     .then_inc(row_a, 1)

                def rows_2():
                    act.wait_ge(row_v, 2 * l + 1)
                    a.activation(rowv[:, R_E, :], rowv[:, R_F, :], ACT.Exp).then_inc(row_a, 1)

                def weights(j):
                    act.wait_ge(dm_ok, 4 * l + j + 1)
                    for h in range(2):
                        a.activation(Wd[:, h, 0:S], Dm[:, h, 0:S], ACT.Exp,
                                     bias=ucol[:, 0, 2 * j + h:2 * j + h + 1])
                        m = a.activation(Wd[:, h, S:S + P], Dm[:, h, S:S + P], ACT.Exp,
                                         bias=ucol[:, 1, 2 * j + h:2 * j + h + 1])
                    m.then_inc(wd_ok, 1)

                def v_copy(j):
                    n = 3 * j
                    done(f"voz{l}", n)
                    u = U[f"voz{l}"] + n
                    for T in range(TT):
                        m = a.activation(vx[:, T, :, 0:S],
                                         pairs[:, u % 2, T, :].rearrange("p (h v) -> p h v", h=2),
                                         ACT.Copy)
                    read(m, u)

                def den_abs(j):
                    act.wait_ge(num_mm, 4 * l + j + 1)
                    a.activation(den4, misc[:, :, S:S + 1].rearrange("p (t h) a -> p t (h a)", t=TT),
                                 ACT.Abs).then_inc(den_ok, 1)

                def o_copy(j):
                    if 4 * l + j:
                        act.wait_ge(hh_ok, 4 * l + j)
                    tokens_copy(f"voz{l}", 3 * j + 1, so, ACT.Sigmoid)

                def z_copy(j):
                    if 4 * l + j:
                        act.wait_ge(hz_ok, 4 * l + j)
                    tokens_copy(f"voz{l}", 3 * j + 2, sz, ACT.Silu)

                def head_hi(j):
                    act.wait_ge(hz_t, 4 * l + j + 1)
                    for k in range(4):
                        m = a.activation(b_hi[:, 4 * j + k, :],
                                         misc[:, k // 2, (k % 2) * S:(k % 2 + 1) * S],
                                         ACT.Identity, scale=col(f"head_norm{l}", 4 * j + k))
                    m.then_inc(mh_hi, 1)

                for m_ in range(16):
                    todo = lru_unit(l, m_)
                    if m_ == 12:
                        todo[7].append(rows_1)
                    if m_ == 13:
                        todo[4].append(rows_2)
                    work(todo)
                for j in range(4):
                    todo = {4: [lambda: weights(j)]}
                    if j:
                        todo[3] = [lambda: z_copy(j - 1)]
                        todo[7] = [lambda: head_hi(j - 1)]
                    work(todo)
                    work({3: [lambda: v_copy(j)]})
                    work({3: [lambda: o_copy(j)], 5: [lambda: den_abs(j)]})
                work({3: [lambda: z_copy(3)], 7: [lambda: head_hi(3)]})
                for j in range(3):
                    run(4); residual_squares(f"wa{l}", j); run(4)
                residual_squares(f"wa{l}", 3)
                squares_done()

        @block.vector
        def _(dve):
            v = nc.vector
            step = Steps(dve, dve_s)
            v.sem_inc(hi_done, RAW_FREE)
            v.sem_inc(lo_done, RAW_FREE)
            for r in range(2):
                v.sem_inc(pair_read[r], PAIR_FREE)
            state = [0]

            def half(count, i):
                dve.wait_ge(hi_done, count)
                v.tensor_tensor(w_lo[:, i % HSLOTS], raw[:, i // 2, 2 * (i % 2):2 * (i % 2) + 2, :],
                                w_hi[:, i % HSLOTS].bitcast(F32), ALU.subtract).then_inc(lo_done, 1)

            def run(n):
                for _ in range(n):
                    half(RAW_FREE + state[0] + 1, state[0] % HALVES)
                    state[0] += 1

            def split_lo(N, c, dst_hi, dst_lo, gain):
                n = 4 * N + c
                dve.wait_ge(n_hi, n + 1)
                for k in range(4):
                    m = v.scalar_tensor_tensor(
                        dst_lo[:, 4 * c + k, :], misc[:, 2 * (n % 2) + k // 2, (k % 2) * S:(k % 2 + 1) * S],
                        col(gain, 4 * c + k), dst_hi[:, 4 * c + k, :].bitcast(F32), ALU.mult, ALU.subtract)
                m.then_inc(n_lo, 1)

            def variance(event):
                dve.wait_ge(squares, event + 1)
                step(v.tensor_reduce(var, sq_part, AX.X, ALU.add))
                step.wait()
                v.tensor_scalar(var, var, 1.0 / D, EPS, ALU.mult, ALU.add).then_inc(var_ok, 1)

            def scale_slice(N, event, c, src, xs):
                n = 4 * N + c
                if c == 0:
                    dve.wait_ge(rstd_ok, event + 1)
                if n >= 2:
                    dve.wait_ge(turned, n - 1)
                for T in range(TT):
                    m = v.tensor_scalar(xs[:, c if N == 3 else n % 2, T, :],
                                        src[:, T, c * COLS:(c + 1) * COLS],
                                        rstd[:, event % 2, T:T + 1], None, ALU.mult)
                m.then_inc(xs_ok, 1)

            dve.wait_ge(consts, 4)
            step(v.tensor_tensor(iota_x, iota_s, iota_t, ALU.bitwise_xor))
            step.wait()
            v.tensor_copy(xor_f[:], iota_x).then_inc(xor_ok, 1)
            for g, wdw in enumerate(POOL_WINDOWS):
                m = v.tensor_scalar(inv[:, g, :], iota_1, float(wdw), None, ALU.min)
            step(m)
            step.wait()
            v.reciprocal(inv, inv).then_inc(inv_ok, 1)
            variance(0)
            dve.wait_ge(consts, 5)
            for l in range(LEVELS - 1):
                v.tensor_scalar(lvl_mask[:, l, :], xor_f[:], float(1 << l), None, ALU.is_ge)
            dve.wait_ge(rows_t, 1)
            for i, n in enumerate(row_tiles):
                m = v.tensor_copy(vecs[:, i, 0:n], misc[:, 0 if i < 4 else 1, (i % 4) * P:(i % 4) * P + n])
            m.then_inc(vecs_ok, 1)
            for c in range(2):
                scale_slice(0, 0, c, x, xs_first)
            dve.wait_ge(vecs_ok, 1)
            v.tensor_tensor(lam_t[5][:, 0, 0:8], cols("lb0", 8), cols("lb1", 8), ALU.subtract)\
             .then_inc(lb_d, 1)
            tile0, at0 = rows_at["lam0"]
            lam_in = vecs[:, tile0:tile0 + 3:2, at0:at0 + 16]
            v.scalar_tensor_tensor(lam_t[0], lam_in, -1.0, lam_in, ALU.mult, ALU.max)\
             .then_inc(lam_d, 1)
            for c in range(2):
                split_lo(0, c, a_hi, a_lo, "norm_mix")
                scale_slice(0, 0, c + 2, x, xs_first)
            dve.wait_ge(lam_a, 1)
            v.tensor_scalar(lam_t[2], lam_t[1], 1.0, None, ALU.add).then_inc(lam_d, 1)
            for c in range(2, 4):
                split_lo(0, c, a_hi, a_lo, "norm_mix")
            variance(1)
            for c in range(2):
                scale_slice(1, 1, c, memx, xs_first)
            run(5)
            for c in range(4):
                split_lo(1, c, b_hi, b_lo, "norm_mem")
                if c < 2:
                    scale_slice(1, 1, c + 2, memx, xs_first)
                if c < 3:
                    run(1)
            dve.wait_ge(lam_a, 2)
            e_, y_, ln_, t4, t5 = lam_t[1], lam_t[2], lam_t[3], lam_t[4], lam_t[5]
            dve.wait_ge(lam_d, 2)
            step(v.tensor_scalar(y_, y_, -1.0, None, ALU.add)); step.wait()
            dve.wait_ge(lb_sig, 1)
            step(v.tensor_scalar(t4, y_, 0.0, None, ALU.is_equal)); step.wait()
            step(v.tensor_tensor(y_, y_, t4, ALU.add)); step.wait()
            step(v.reciprocal(y_, y_)); step.wait()
            step(v.tensor_tensor(ln_, ln_, e_, ALU.mult)); step.wait()
            step(v.tensor_tensor(ln_, ln_, y_, ALU.mult)); step.wait()
            step(v.tensor_tensor(t4, t4, e_, ALU.mult)); step.wait()
            step(v.tensor_tensor(ln_, ln_, t4, ALU.add)); step.wait()
            step(v.tensor_scalar(t5, lam_in, -1.0, 0.0, ALU.mult, ALU.max)); step.wait()
            step(v.tensor_tensor(ln_, ln_, t5, ALU.add)); step.wait()
            v.tensor_scalar(lam_c, ln_, -LRU_C, None, ALU.mult)
            v.tensor_scalar(lam_p, ln_, LRU_C, None, ALU.mult).then_inc(lam_ok, 1)
            run(8)
            run(8)

            def forget(j):
                copied(dve, U["f"] + j)
                dve.wait_ge(lb_sig, 1)
                for h in range(4 * j, 4 * j + 4):
                    v.tensor_scalar(kb[:, h, :], kb[:, h, :], omlb[:, h:h + 1], None, ALU.mult)
                    m = v.tensor_scalar(ab[:, h, :], ab[:, h, :], omlb[:, h:h + 1], lb[:, h:h + 1],
                                        ALU.mult, ALU.add)
                step(m)
                step.wait()
                v.tensor_scalar(ab[:, 4 * j:4 * j + 4, :], ab[:, 4 * j:4 * j + 4, :], 1e-19, None,
                                ALU.max).then_inc(f_ok, 1)

            def decay_sums(j):
                dve.wait_ge(logf_ok, j + 1)
                for h in range(4 * j, 4 * j + 4):
                    m = v.tensor_tensor_scan(ab[:, h, :], ones[:], ab[:, h, :], 0.0, ALU.mult, ALU.add)
                m.then_inc(scan_ok, 1)

            run(4); forget(0); run(3); decay_sums(0); run(1)
            run(4); forget(1); run(3); decay_sums(1); run(1)
            run(8)

            def level_views(l):
                B = 1 << l
                return B, HEADS * S // (2 * B), [z.rearrange("p h (m two b) -> p (h m) two b", two=2, b=B)
                                                 for z in (X, ab, qb)]

            def sub_odd(l):
                B, n, (Xv, av, _) = level_views(l)
                v.tensor_tensor(Xv[:, :, 1, :], av[:, :, 1, :],
                                av[:, :, 0, B - 1:B].to_broadcast([P, n, B]), ALU.subtract)\
                 .then_inc(sub_v, 1)

            def mul_odd(l):
                B, n, (Xv, _, qv) = level_views(l)
                dve.wait_ge(lvl_exp, l + 1)
                v.tensor_tensor(Xv[:, :, 1, :], Xv[:, :, 1, :], qv[:, :, 1, :], ALU.mult)\
                 .then_inc(mul_v, 1)

            def diagonal():
                dve.wait_ge(lvl_mm, 1)
                eye = ident[:].unsqueeze(1).to_broadcast([P, HEADS, P])
                for T in range(TT):
                    m = v.tensor_tensor(scb[:, 2 * T], misc[:, 2 * T:2 * T + 2]
                                        .rearrange("p b (h t) -> p (b h) t", h=4), eye, ALU.mult)
                m.then_inc(lvl_sel, 1)

            def select(l):
                dve.wait_ge(lvl_mm, l + 2)
                if l == LEVELS - 1:
                    v.tensor_copy(scb[:, 1], misc[:, 0:2].rearrange("p b (h t) -> p (b h) t", h=4))\
                     .then_inc(lvl_sel, 1)
                    return
                dve.wait_ge(lvl_sel, l + 1)
                mask = lvl_mask[:, l, :].unsqueeze(1).to_broadcast([P, HEADS, P])
                for T in range(TT):
                    m = v.copy_predicated(scb[:, 2 * T], mask, misc[:, 2 * T:2 * T + 2]
                                          .rearrange("p b (h t) -> p (b h) t", h=4))
                m.then_inc(lvl_sel, 1)

            dve.wait_ge(scan_ok, 2)
            for l in range(LEVELS):
                run(1)
                sub_odd(l)
                run(1)
                if l == 0:
                    diagonal()
                    copied(dve, U["q"] + 1)
                mul_odd(l)
                run(2)
                select(l)
            run(8)
            dve.wait_ge(o_sq, 1)
            step(v.tensor_reduce(ss16, Xflat.rearrange("p (a b) -> p a b", a=16), AX.X, ALU.add))
            step.wait()
            v.tensor_scalar(ss16, ss16, 1.0 / P, EPS, ALU.mult, ALU.add).then_inc(o_ss, 1)
            run(2)
            dve.wait_ge(o_rs, 1)
            step(v.tensor_tensor(yo, misc[:].rearrange("p b (h c) -> p (b h) c", h=4),
                                 rs16.unsqueeze(2).to_broadcast([P, 16, P]), ALU.mult))
            run(1)
            copied(dve, U["g"] + 1)
            step.wait()
            yt = yo.rearrange("p (t h) c -> p t (h c)", t=TT)
            v.tensor_tensor(yt, yt, gb, ALU.mult).then_inc(o_y, 1)
            run(5)
            run(5)
            dve.wait_ge(m_hi, 1)
            v.scalar_tensor_tensor(a_lo[:, 8:16, :].rearrange("p k t -> p (k t)"),
                                   misc[:].rearrange("p b c -> p (b c)"), col("hgrn_norm"),
                                   a_hi[:, 8:16, :].bitcast(F32).rearrange("p k t -> p (k t)"),
                                   ALU.mult, ALU.subtract).then_inc(m_lo, 1)
            run(3)
            run(5)
            dve.wait_ge(m_hi, 2)
            for k in range(8):
                m = v.scalar_tensor_tensor(a_lo[:, k, :], misc[:, k // 2, (k % 2) * S:(k % 2 + 1) * S],
                                           col("pool_scale", k), a_hi[:, k, :].bitcast(F32),
                                           ALU.mult, ALU.subtract)
            m.then_inc(m_lo, 1)
            run(3)
            run(4 * HALVES)

            def add_unit(name, j):
                u = U[name] + j
                finished(dve, H[name] + (j + 1) * HALVES)
                xs = x[:, :, j * COLS:(j + 1) * COLS]
                v.tensor_tensor(xs, pairs[:, u % 2], xs, ALU.add).then_inc(pair_read[u % 2], 1)

            run(8)
            dve.wait_ge(x_back, 16)
            for j in range(3):
                run(3); add_unit("wout", j); run(5)
            add_unit("wout", 3)

            def renorm(N, event, gain, xs=xs_late):
                variance(event)
                for c in range(2):
                    scale_slice(N, event, c, x, xs)
                for c in range(4):
                    split_lo(N, c, a_hi, a_lo, gain)
                    if c < 2:
                        scale_slice(N, event, c + 2, x, xs)

            renorm(2, 2, "norm_xattn")

            def soft_max(j):
                dve.wait_ge(att_sc, j + 1)
                step(v.tensor_reduce(mx, misc[:, 0].rearrange("p (t m) -> p t m", t=TT), AX.X, ALU.max))
                step.wait()
                v.tensor_scalar(nmx, mx, -XD ** -0.5, None, ALU.mult).then_inc(att_max, 1)

            def soft_norm(j):
                dve.wait_ge(att_exp, j + 1)
                step(v.reciprocal(rsum, psumv))
                step.wait()
                for T in range(TT):
                    m = v.tensor_scalar(prob[:, T, :], prob[:, T, :], rsum[:, T:T + 1], None, ALU.mult)
                m.then_inc(att_p, 1)

            def attended_lo(j):
                dve.wait_ge(att_hi, j + 1)
                v.tensor_tensor(b_lo[:, 4 * j:4 * j + 4, :],
                                misc[:, 2:4].rearrange("p b (f t) -> p (b f) t", f=2),
                                b_hi[:, 4 * j:4 * j + 4, :].bitcast(F32), ALU.subtract)\
                 .then_inc(att_lo, 1)

            run(8)
            for j in range(1, XHEADS):
                if j >= 2:
                    run(1); attended_lo(j - 2); run(3)
                else:
                    run(4)
                soft_max(j - 1); run(1); soft_norm(j - 1); run(3)
            attended_lo(2)
            run(2); soft_max(3); run(1); soft_norm(3); run(4); attended_lo(3); run(1)
            for j in range(3):
                run(3); add_unit("wo", j); run(5)
            add_unit("wo", 3)
            renorm(3, 3, "norm_ffn", xs_all)

            def routing():
                dve.wait_ge(rt_mm, 1)
                def s1(ins):
                    step(ins)
                    step.wait()
                def b4(ap):
                    return ap.to_broadcast([P, TT, 4])
                s1(v.tensor_copy(rt_l, misc[:, 0, 0:40].rearrange("p (t c) -> p t c", t=TT)))
                gl, el = rt_l[:, :, 0:4], rt_l[:, :, 4:20]
                s1(v.tensor_reduce(rt_m, gl, AX.X, ALU.max))
                v.tensor_tensor(rt_gd, gl, b4(rt_m.unsqueeze(2)), ALU.subtract).then_inc(rt_x, 1)

                def first_max(dst, src, m):
                    s1(v.tensor_tensor(dst, src, b4(m.unsqueeze(2)), ALU.is_equal))
                    s1(v.tensor_tensor(dst, dst, b4_rank, ALU.mult))
                    s1(v.tensor_reduce(rt_m2, dst, AX.X, ALU.max))
                    s1(v.tensor_tensor(dst, dst, b4(rt_m2.unsqueeze(2)), ALU.is_equal))

                for i in range(4):
                    m = v.memset(rt_rank[:, i:i + 1], float(4 - i))
                step(m)
                step.wait()
                b4_rank = rt_rank.unsqueeze(1).to_broadcast([P, TT, 4])
                first_max(rt_og, gl, rt_m)
                for g in range(4):
                    o = rt_og[:, :, g:g + 1].to_broadcast([P, TT, 4])
                    if g == 0:
                        s1(v.tensor_tensor(rt_sel, el[:, :, 0:4], o, ALU.mult))
                    else:
                        s1(v.tensor_tensor(rt_t, el[:, :, 4 * g:4 * g + 4], o, ALU.mult))
                        s1(v.tensor_tensor(rt_sel, rt_sel, rt_t, ALU.add))
                s1(v.tensor_reduce(rt_m, rt_sel, AX.X, ALU.max))
                first_max(rt_o1, rt_sel, rt_m)
                s1(v.tensor_scalar(rt_t, rt_o1, -1.0, 1.0, ALU.mult, ALU.add))
                s1(v.tensor_tensor(rt_sel, rt_sel, rt_t, ALU.mult))
                s1(v.tensor_scalar(rt_t, rt_o1, -3e38, None, ALU.mult))
                s1(v.tensor_tensor(rt_sel, rt_sel, rt_t, ALU.add))
                s1(v.tensor_reduce(rt_m3, rt_sel, AX.X, ALU.max))
                v.tensor_tensor(rt_dm, rt_m3, rt_m, ALU.subtract).then_inc(rt_x, 1)
                first_max(rt_o2, rt_sel, rt_m3)
                s1(v.tensor_tensor(rt_t, rt_o1, rt_o2, ALU.add))
                for g in range(4):
                    m = v.tensor_tensor(chosen[:, :, 4 * g:4 * g + 4], rt_t,
                                        rt_og[:, :, g:g + 1].to_broadcast([P, TT, 4]), ALU.mult)
                m.then_inc(chosen_ok, 1)
                dve.wait_ge(rt_e, 2)
                s1(v.tensor_reduce(rt_pg, rt_ge, AX.X, ALU.add))
                s1(v.reciprocal(rt_pg, rt_pg))
                s1(v.tensor_scalar(rt_w1, rt_w, 1.0, None, ALU.add))
                s1(v.reciprocal(rt_w1, rt_w1))
                s1(v.tensor_tensor(rt_w1, rt_w1, rt_pg, ALU.mult))
                s1(v.tensor_tensor(rt_w2, rt_w1, rt_w, ALU.mult))
                s1(v.tensor_tensor(rt_o1, rt_o1, b4(rt_w1.unsqueeze(2)), ALU.mult))
                s1(v.tensor_tensor(rt_o2, rt_o2, b4(rt_w2.unsqueeze(2)), ALU.mult))
                s1(v.tensor_tensor(rt_o1, rt_o1, rt_o2, ALU.add))
                for g in range(4):
                    m = v.tensor_tensor(comb[:, :, 4 * g:4 * g + 4], rt_o1,
                                        rt_og[:, :, g:g + 1].to_broadcast([P, TT, 4]), ALU.mult)
                m.then_inc(comb_ok, 1)
                dve.wait_ge(rank_mm, 1)
                s1(v.tensor_reduce(fullest, misc[:, 1, 32:48], AX.X, ALU.max))
                v.tensor_scalar(crowded, fullest, -float(P), 0.0, ALU.add, ALU.max)\
                 .then_inc(crowd_ok, 1)
                v.tensor_tensor(slot_of[:, :, 0:EXPERTS],
                                misc[:, 1, 0:32].rearrange("p (t e) -> p t e", t=TT), chosen,
                                ALU.mult).then_inc(slots_ok, 1)

            def choose(e, count):
                if count is not None:
                    dve.wait_ge(place_mm, count)
                for T in range(TT):
                    m = v.tensor_scalar(pick_r[:, T, :], slot_f, slot_of[:, T, e], None, ALU.is_equal)
                m.then_inc(pick_ok, 1)

            def gathered_lo(e, c):
                dve.wait_ge(pick_hi, e * 4 + (c + 1))
                for k in range(4):
                    m = v.scalar_tensor_tensor(
                        a_lo[:, 4 * c + k, :], misc[:, 2 * (c % 2) + k // 2, (k % 2) * S:(k % 2 + 1) * S],
                        col("norm_ffn", 4 * c + k), a_hi[:, 4 * c + k, :].bitcast(F32), ALU.mult,
                        ALU.subtract)
                m.then_inc(pick_lo, 1)

            def hidden_lo(e):
                dve.wait_ge(hid_hi, e + 1)
                v.tensor_tensor(b_lo[:, 0:4, :].rearrange("p k t -> p (k t)"),
                                misc[:, 0:2].rearrange("p b c -> p (b c)"),
                                b_hi[:, 0:4, :].bitcast(F32).rearrange("p k t -> p (k t)"),
                                ALU.subtract).then_inc(hid_lo, 1)

            def add_expert(r, n, e, before):
                dve.wait_ge(pair_read[r], before)
                for T in range(TT):
                    xs = x[:, T, n * COLS:(n + 1) * COLS]
                    m = v.scalar_tensor_tensor(xs, pairs[:, r, T, :], comb[:, T, e], xs,
                                               ALU.mult, ALU.add)
                m.then_inc(pair_read[r], 1)

            run(4)
            for c in range(SPLIT):
                dve.wait_ge(xt_h, c + 1)
                v.tensor_tensor(xt_lo[c], xs_all[:, c], xt_hi[c].bitcast(F32), ALU.subtract)\
                 .then_inc(xt_l, 1)
            dve.wait_ge(slots_in, 1)
            v.tensor_copy(slot_f, slot_i)
            v.tensor_scalar(upto, causal[:], -0.5, None, ALU.is_ge)
            v.memset(slot_of[:, :, EXPERTS:EXPERTS + 1], 0.0)
            routing()
            dve.wait_ge(slots_ok, 1)
            choose(slice(0, 1), None)
            for c in range(4):
                gathered_lo(0, c)
            run(4)
            choose(slice(1, 2), 1)
            run(4); gathered_lo(1, 0)
            run(2); gathered_lo(1, 1)
            run(2); gathered_lo(1, 2)
            h0 = H["moe"]
            u0 = U["moe"]
            dve.wait_ge(comb_ok, 1)
            with dve.Fori(0, EXPERTS - 1) as e:
                def halves(first, n):
                    for i in range(first, first + n):
                        half(e * 24 + (RAW_FREE + h0 + i + 1), i % HALVES)

                def one_down(n):
                    dve.wait_ge(used, e * 24 + (h0 + 8 + 4 * n + 2 + HALF_FREE))
                    add_expert(0, n, bass.ds(e, 1), e * 5 + (MOE_READS + 1 + n))

                halves(0, 4)
                dve.wait_ge(used, e * 24 + (h0 + HALF_FREE))
                dve.wait_ge(pair_read[0], e * 5 + MOE_READS)
                v.tensor_tensor(hid, gs, pairs[:, 1].rearrange("p t c -> p (t c)"), ALU.mult)\
                 .then_inc(pair_read[1], 1)
                gathered_lo(e + 1, 3)
                halves(4, 4); hidden_lo(e)
                halves(8, 2); choose(bass.ds(e + 2, 1), e + 2)
                halves(10, 3); one_down(0)
                halves(13, 3); gathered_lo(e + 2, 0)
                halves(16, 1); one_down(1)
                halves(17, 3); gathered_lo(e + 2, 1)
                halves(20, 1); one_down(2)
                halves(21, 3); gathered_lo(e + 2, 2)
                one_down(3)
            state[0] = H["down"]
            gathered_lo(EXPERTS, 3)
            finished(dve, H["down"])
            dve.wait_ge(pair_read[0], U["down"] // 2 + PAIR_FREE)
            v.tensor_tensor(hid, gs, pairs[:, 1].rearrange("p t c -> p (t c)"), ALU.mult)\
             .then_inc(pair_read[1], 1)
            dve.wait_ge(pair_read[1], EXPERTS - 1 + MOE_READS)
            v.sem_inc(pair_read[1], 4 * (EXPERTS - 1))
            hidden_lo(EXPERTS - 1)
            run(4)
            for n in range(4):
                if n < 2:
                    run(2)
                u = U["down"] + n
                finished(dve, H["down"] + 2 * (n + 1))
                add_expert(u % 2, n, slice(EXPERTS - 1, EXPERTS), u // 2 + PAIR_FREE)

            def scale_rows(event, gain, loads):
                variance(event)
                dve.wait_ge(rstd_ok, event + 1)
                dve.wait_ge(gain_in, 16 * loads)
                for T in range(TT):
                    v.scalar_tensor_tensor(x[:, T, :], x[:, T, :], rstd[:, event % 2, T:T + 1], gain,
                                           ALU.mult, ALU.mult).then_inc(scaled, 1)

            scale_rows(4, gain_b, 1)

            dve.wait_ge(lam_ok, 1)

            def conv_tile(l, i, f):
                src = XP[:, f, :]
                name, n = (f"lru_conv{l}", 4 * i + f) if i < 4 else (f"qk_conv{l}", 4 * (i - 4) + f)
                if f == 0:
                    if i < 4:
                        copied(dve, U[f"lru{l}"] + 2 * i)
                        if 4 * l + i:
                            dve.wait_ge(ui_ok, 4 * l + i)
                        if l and i == 0:
                            dve.wait_ge(mh_lo, 4 * l)
                    else:
                        copied(dve, U[f"qk{l}"] + i - 4)
                        if i == 4:
                            dve.wait_ge(ui_ok, 4 * (l + 1))
                        else:
                            dve.wait_ge(qk_ok, 4 * l + i - 4)
                o = xc[:, f, :]
                if i < 4:
                    step(v.tensor_scalar(o, src[:, 0:S], col(name, n), col(f"lru_b{l}", 4 * i + f),
                                         ALU.mult, ALU.add))
                else:
                    step(v.tensor_scalar(o, src[:, 0:S], col(name, n), None, ALU.mult))
                for w in range(1, CONV_W):
                    step.wait()
                    m = v.scalar_tensor_tensor(o, src[:, w:w + S], col(name, 16 * w + n), o,
                                               ALU.mult, ALU.add)
                    if w < CONV_W - 1:
                        step(m)
                if f == 3:
                    m.then_inc(conv_ok, 1)

            def one_minus_a2(l, j):
                dve.wait_ge(a2_ok, 4 * l + j + 1)
                v.scalar_tensor_tensor(Tb, Rb, 1.0, Tb, ALU.add, ALU.mult).then_inc(om_ok, 1)

            def recur(l, j):
                n = 4 * l + j
                dve.wait_ge(sq_ok, n + 1)
                dve.wait_ge(ui_ok, n + 1)
                step(v.tensor_tensor(Tb, Tb, Ib, ALU.mult))
                step.wait()
                for k in range(4):
                    m = v.tensor_tensor_scan(Rb[:, k, :], Ab[:, k, :], Tb[:, k, :], 0.0, ALU.mult,
                                             ALU.add)
                m.then_inc(h_ok, 1)

            def y_lo(l, j):
                n = 4 * l + j
                dve.wait_ge(lru_hi, n + 1)
                v.tensor_tensor(b_lo[:, 4 * j:4 * j + 4, :], Zb, b_hi[:, 4 * j:4 * j + 4, :].bitcast(F32),
                                ALU.subtract).then_inc(lru_lo, 1)

            def rows_v(l):
                dve.wait_ge(row_a, 2 * l + 1)
                def s1(ins):
                    step(ins)
                    step.wait()
                s1(v.scalar_tensor_tensor(rowv[:, R_B, :], rowv[:, R_F, :], 0.0, rowv[:, R_A, :],
                                          ALU.min, ALU.subtract))
                s1(v.tensor_tensor_scan(rowv[:, R_B, :], ones[0:8, :], rowv[:, R_B, :], 0.0,
                                        ALU.mult, ALU.add))
                s1(v.tensor_tensor(rowv[:, R_U, :], rowv[:, R_I, :], rowv[:, R_B, :], ALU.subtract))
                s1(v.tensor_tensor_scan(rowv[:, R_M, :], ones[0:8, :], rowv[:, R_U, :], 0.0,
                                        ALU.mult, ALU.max))
                s1(v.tensor_tensor(rowv[:, R_B, :], rowv[:, R_B, :], rowv[:, R_M, :], ALU.add))
                v.tensor_scalar(rowv[:, R_F, :], rowv[:, R_B, :], -1.0, 85.0, ALU.mult, ALU.min)\
                 .then_inc(row_v, 1)
                v.tensor_scalar(rowv[:, R_M, :], rowv[:, R_M, :], -1.0, None, ALU.mult)\
                 .then_inc(row_v, 1)

            def decays(l, j):
                g = 4 * l + j
                dve.wait_ge(bc_mm, g + 1)
                if g:
                    dve.wait_ge(wd_ok, g)
                m2 = misc[:, 0].rearrange("p (h t) -> p h t", h=2)
                cm = causal[:].unsqueeze(1).to_broadcast([P, 2, P])
                v.tensor_tensor(Dm[:, :, 0:P], m2[:, :, 0:P], cm, ALU.add)
                v.tensor_copy(Dm[:, :, P:S], m2[:, :, P:S])
                v.tensor_tensor(Dm[:, :, S:S + P], m2[:, :, P:S], cm, ALU.add).then_inc(dm_ok, 1)

            def weigh(l, j):
                g = 4 * l + j
                dve.wait_ge(wd_ok, g + 1)
                if g:
                    dve.wait_ge(num_mm, g)
                for h in range(2):
                    m = v.scalar_tensor_tensor(scW[:, h, :], misc[:, 1 + h, 0:384], DK ** -0.5,
                                               Wd[:, h, :], ALU.mult, ALU.mult)
                m.then_inc(scw_ok, 1)

            def head_values(l, j):
                g = 4 * l + j
                def s1(ins):
                    step(ins)
                    step.wait()
                dve.wait_ge(den_ok, g + 1)
                s1(v.tensor_tensor(den4, den4, ecol[:, :, 2 * j:2 * j + 2], ALU.max))
                s1(v.reciprocal(rden4, den4))
                copied(dve, U[f"voz{l}"] + 3 * j + 1)
                if g:
                    dve.wait_ge(hz_t, g)
                for T in range(TT):
                    for h in range(2):
                        m = v.scalar_tensor_tensor(hh[:, T, h * S:(h + 1) * S], misc[:, 2 * T + h, 0:S],
                                                   rden4[:, T, h:h + 1], so[:, T, h * S:(h + 1) * S],
                                                   ALU.mult, ALU.mult)
                m.then_inc(hh_ok, 1)
                dve.wait_ge(hh_ok, g + 1)
                for i in range(4):
                    m = v.bn_stats(bn[:, i, :], hh[:, i // 2, (i % 2) * S:(i % 2 + 1) * S])
                s1(m)
                for i in range(4):
                    m = v.bn_aggr(mv4[:, i, :], bn[:, i, :])
                s1(m)
                v.tensor_scalar(ve4.unsqueeze(2), mv4[:, :, 1:2], EPS, None, ALU.add).then_inc(ve_ok, 1)

            def head_norms(l, j):
                g = 4 * l + j
                dve.wait_ge(rs_ok, g + 1)
                for i in range(4):
                    o = hh[:, i // 2, (i % 2) * S:(i % 2 + 1) * S]
                    m = v.tensor_scalar(o, o, mv4[:, i, 0:1], rs4[:, i:i + 1], ALU.subtract, ALU.mult)
                m.then_inc(hn_ok, 1)

            def head_gate(l, j):
                g = 4 * l + j
                dve.wait_ge(hn_ok, g + 1)
                copied(dve, U[f"voz{l}"] + 3 * j + 2)
                v.tensor_tensor(hh, hh, sz, ALU.mult).then_inc(hz_ok, 1)

            def head_lo(l, j):
                g = 4 * l + j
                dve.wait_ge(mh_hi, g + 1)
                for k in range(4):
                    m = v.scalar_tensor_tensor(b_lo[:, 4 * j + k, :],
                                               misc[:, k // 2, (k % 2) * S:(k % 2 + 1) * S],
                                               col(f"head_norm{l}", 4 * j + k),
                                               b_hi[:, 4 * j + k, :].bitcast(F32), ALU.mult, ALU.subtract)
                m.then_inc(mh_lo, 1)

            def work(todo):
                for i in range(9):
                    for f in todo.get(i, []):
                        f()
                    if i < 8:
                        run(1)

            for l in range(LAYERS):
                renorm(4 + l, 5 + l, f"norm{l}")
                for m_ in range(16):
                    todo = {i: [] for i in range(9)}
                    if m_ <= 7 and m_ % 2 == 1 or 9 <= m_ <= 12:
                        i = m_ // 2 if m_ <= 7 else m_ - 5
                        for f in range(4):
                            todo[4 + f].append(lambda f=f: conv_tile(l, i, f))
                    if 3 <= m_ <= 9 and m_ % 2 == 1:
                        j = (m_ - 3) // 2
                        todo[1].append(lambda: one_minus_a2(l, j))
                        todo[3].append(lambda: recur(l, j))
                        todo[8].append(lambda: y_lo(l, j))
                    if m_ == 12:
                        def if_out():
                            dve.wait_ge(if_mm, l + 1)
                            v.tensor_copy(igfg, misc[:, 0, 0:32].rearrange("p (t c) -> p t c", t=TT))\
                             .then_inc(if_sb, 1)
                        todo[3].append(if_out)
                    if m_ >= 13:
                        todo[3].append(lambda: add_unit(f"wb{l}", m_ - 13))
                    if m_ == 13:
                        todo[1].append(lambda: rows_v(l))
                    if m_ == 14:
                        def cols_out():
                            dve.wait_ge(col_t, l + 1)
                            v.tensor_copy(uecol.rearrange("p g t h -> p (g t h)"), misc[:, 2, 0:32])\
                             .then_inc(col_ok, 1)
                        todo[4].append(cols_out)
                    work(todo)
                for j in range(4):
                    todo = {3: [lambda: decays(l, j)], 6: [lambda: weigh(l, j)]}
                    if j:
                        todo[1] = [lambda: head_norms(l, j - 1)]
                        todo[4] = [lambda: head_gate(l, j - 1)]
                        todo[7] = [lambda: head_lo(l, j - 1)]
                    else:
                        todo[3].insert(0, lambda: add_unit(f"wb{l}", 3))
                    work(todo)
                    work({})
                    work({6: [lambda: head_values(l, j)]})
                work({1: [lambda: head_norms(l, 3)], 4: [lambda: head_gate(l, 3)],
                      7: [lambda: head_lo(l, 3)]})
                for j in range(3):
                    run(3); add_unit(f"wa{l}", j); run(5)
                add_unit(f"wa{l}", 3)
            scale_rows(7, gain_e, 2)


_INS = ["x", "mem", "norm_mix", "w_in", "pool_w", "pool_scale", "hgrn_lb_logits", "hgrn_norm", "w_out",
        "norm_xattn", "norm_mem", "xattn_wq", "xattn_wk", "xattn_wv", "xattn_wo", "norm_ffn",
        "router_group", "router_expert", "w_gate", "w_up", "w_down", "norm_final", "norm_g_2", "w_in_2",
        "i_bias_2", "f_bias_2", "qk_conv_2", "head_norm_g_2", "lru_conv_w_2", "lru_conv_b_2", "w_a_2",
        "b_a_2", "w_x_2", "b_x_2", "lam_2", "w_out_2", "final_g_2"]



def kernel(**inputs):
    import numpy as _np
    import concourse.bacc as _bacc
    from concourse import mybir as _mybir
    from concourse.bass_utils import run_bass_kernel_spmd as _run

    nc = _bacc.Bacc("TRN2", target_bir_lowering=False, num_devices=1)
    arrays, args = {}, {}
    for name in _INS:
        a = _np.ascontiguousarray(inputs[name])
        arrays[f"in_{name}_dram"] = a
        args[name] = nc.dram_tensor(f"in_{name}_dram", a.shape, _mybir.dt.from_np(a.dtype),
                                    kind="ExternalInput").ap()
    out = nc.dram_tensor("out_0_dram", (1, S, D), F32, kind="ExternalOutput").ap()
    program(nc, args, out)
    r = _run(nc, [arrays], core_ids=[0])
    return r.results[0]["out_0_dram"]
```
